# Optimizing a Trainium2 kernel written in Bass

```python
import jax
import jax.numpy as jnp
from jax import lax
import numpy as np

D_MODEL = 2048
BATCH = 1
SEQ = 256
DEPTH = 1

Q_BLOCK = 128
SWA_HEADS = 8
SWA_KV_HEADS = 2
SWA_HEAD_DIM = 64
SWA_WINDOW = 128
SB_HEADS = 4
SB_HEAD_DIM = 128
NSA_HEADS = 8
NSA_KV_HEADS = 2
NSA_HEAD_DIM = 64
CMP_BLOCK = 32
CMP_STRIDE = 16
CMP_HIDDEN = 256
SEL_BLOCK = 64
SEL_TOPK = 8
NSA_WINDOW = 512
D_FF = -(-8 * D_MODEL // (3 * 256)) * 256

NEG = -1e30
SEL_FORCE = 1e9
RMS_EPS = 1e-6

IN_SPLITS = (
    SWA_HEADS * SWA_HEAD_DIM, SWA_KV_HEADS * SWA_HEAD_DIM, SWA_KV_HEADS * SWA_HEAD_DIM,
    SB_HEADS * SB_HEAD_DIM, SB_HEADS * SB_HEAD_DIM, SB_HEADS * SB_HEAD_DIM,
    NSA_HEADS * NSA_HEAD_DIM,
    NSA_KV_HEADS * NSA_HEAD_DIM, NSA_KV_HEADS * NSA_HEAD_DIM,
    NSA_KV_HEADS * NSA_HEAD_DIM, NSA_KV_HEADS * NSA_HEAD_DIM,
    NSA_KV_HEADS * NSA_HEAD_DIM, NSA_KV_HEADS * NSA_HEAD_DIM,
    3 * NSA_HEADS,
    3 * D_MODEL,
)
N_IN = sum(IN_SPLITS)

kernel_name = "hybrid_swa_stickbreak_nsa_block"

def rms_norm(x, g):
    xf = x.astype(jnp.float32)
    y = xf * lax.rsqrt(jnp.mean(xf * xf, axis=-1, keepdims=True) + RMS_EPS)
    return (y * g.astype(jnp.float32)).astype(x.dtype)

def alibi_slopes(n):
    return jnp.exp2(-8.0 * jnp.arange(1, n + 1, dtype=jnp.float32) / n)

def split_cols(y, sizes):
    out, start = [], 0
    for n in sizes:
        out.append(y[..., start:start + n])
        start += n
    return out

def masked_softmax(s, mask):
    s = jnp.where(mask, s, NEG)
    m = jnp.max(s, axis=-1, keepdims=True)
    p = jnp.where(mask, jnp.exp(s - m), 0.0)
    return p / jnp.maximum(jnp.sum(p, axis=-1, keepdims=True), 1e-30)

def banded_kv(t, n_prev):
    B, S, G, d = t.shape
    nb = S // Q_BLOCK
    tp = jnp.pad(t, ((0, 0), (n_prev * Q_BLOCK, 0), (0, 0), (0, 0)))
    tb = tp.reshape(B, nb + n_prev, Q_BLOCK, G, d)
    return jnp.concatenate([tb[:, i:i + nb] for i in range(n_prev + 1)], axis=2)

def swa_attention(q, k, v, sinks):
    B, S, G, R, d = q.shape
    nb = S // Q_BLOCK
    n_prev = -(-SWA_WINDOW // Q_BLOCK)
    L = (n_prev + 1) * Q_BLOCK
    qb = q.reshape(B, nb, Q_BLOCK, G, R, d)
    kb = banded_kv(k, n_prev)
    vb = banded_kv(v, n_prev)
    s = jnp.einsum('bnqgrd,bnkgd->bngrqk', qb, kb).astype(jnp.float32) * (d ** -0.5)
    i = jnp.arange(Q_BLOCK)
    j = jnp.arange(L)
    dist = i[:, None] - j[None, :] + n_prev * Q_BLOCK
    key_pos = jnp.arange(nb)[:, None] * Q_BLOCK - n_prev * Q_BLOCK + j[None, :]
    mask = ((dist >= 0) & (dist < SWA_WINDOW))[None] & (key_pos >= 0)[:, None, :]
    slopes = alibi_slopes(G * R).reshape(G, R, 1, 1)
    s = s - slopes * dist.astype(jnp.float32)
    s = jnp.where(mask[None, :, None, None], s, NEG)
    sink = sinks.astype(jnp.float32).reshape(1, 1, G, R, 1, 1)
    m = jnp.maximum(jnp.max(s, axis=-1, keepdims=True), sink)
    p = jnp.exp(s - m)
    p = p / (jnp.sum(p, axis=-1, keepdims=True) + jnp.exp(sink - m))
    o = jnp.einsum('bngrqk,bnkgd->bnqgrd', p.astype(v.dtype), vb)
    return o.reshape(B, S, G * R * d)

def stick_breaking(q, k, v):
    B, S, H, d = q.shape
    f32 = jnp.float32
    nb = S // Q_BLOCK
    n_pair = (nb + 1) // 2
    scale = d ** -0.5
    to_blocks = lambda t: t.reshape(B, nb, Q_BLOCK, H, d).transpose(1, 0, 3, 2, 4)
    qb, kb, vb = to_blocks(q), to_blocks(k), to_blocks(v)
    i = jnp.arange(Q_BLOCK)
    later = (i[:, None] > i[None, :]).astype(f32)

    def block_pair(qi, ki, ls, acc):
        qt = lax.dynamic_index_in_dim(qb, qi, 0, keepdims=False)
        kt = lax.dynamic_index_in_dim(kb, ki, 0, keepdims=False)
        vt = lax.dynamic_index_in_dim(vb, ki, 0, keepdims=False)
        z = jnp.einsum('bhqd,bhkd->bhqk', qt, kt).astype(f32) * scale
        mask = (ki * Q_BLOCK + i)[None, :] < (qi * Q_BLOCK + i)[:, None]
        log_fail = jnp.where(mask, jax.nn.log_sigmoid(-z), 0.0)
        log_surv = ls[..., None] + log_fail @ later
        a = jnp.where(mask, jnp.exp(jax.nn.log_sigmoid(z) + log_surv), 0.0)
        acc = acc + jnp.einsum('bhqk,bhkd->bhqd', a.astype(vt.dtype), vt).astype(f32)
        return ls + jnp.sum(log_fail, axis=-1), acc

    def pair(p):
        q_a = p
        q_b = nb - 1 - p

        def step(carry, j):
            ls_a, acc_a, ls_b, acc_b = carry
            is_a = j <= p
            qi = jnp.where(is_a, q_a, q_b)
            ki = jnp.where(is_a, p - j, nb - j)
            ls, acc = block_pair(qi, ki, jnp.where(is_a, ls_a, ls_b), jnp.where(is_a, acc_a, acc_b))
            new = (jnp.where(is_a, ls, ls_a), jnp.where(is_a, acc, acc_a),
                   jnp.where(is_a, ls_b, ls), jnp.where(is_a, acc_b, acc))
            return new, None

        ls0 = jnp.zeros((B, H, Q_BLOCK), f32)
        acc0 = jnp.zeros((B, H, Q_BLOCK, d), f32)
        (_, acc_a, _, acc_b), _ = lax.scan(step, (ls0, acc0, ls0, acc0), jnp.arange(nb + 1))
        return acc_a, acc_b

    out_a, out_b = lax.map(pair, jnp.arange(n_pair))
    o = jnp.concatenate([out_a, out_b[::-1][2 * n_pair - nb:]], axis=0)
    return o.transpose(1, 0, 3, 2, 4).reshape(B, S, H * d).astype(q.dtype)

def compress_blocks(t, pe, w1, w2):
    B, S, G, d = t.shape
    n_cmp = (S - CMP_BLOCK) // CMP_STRIDE + 1
    idx = jnp.arange(n_cmp)[:, None] * CMP_STRIDE + jnp.arange(CMP_BLOCK)[None, :]
    blk = t[:, idx] + pe[:, None, :]
    blk = blk.transpose(0, 1, 3, 2, 4).reshape(B, n_cmp, G, CMP_BLOCK * d)
    return jax.nn.gelu(blk @ w1) @ w2

def gather_rows(src, idx):
    return jax.vmap(jax.vmap(lambda a, i: a[i]))(src, idx)

def nsa_attention(q, gates, k_c, v_c, k_s, v_s, k_w, v_w,
                  pe_k, w1_k, w2_k, pe_v, w1_v, w2_v):
    B, S, G, R, d = q.shape
    dt = q.dtype
    nb = S // Q_BLOCK
    scale = d ** -0.5
    slopes = alibi_slopes(G * R).reshape(G, R, 1, 1)

    kc = compress_blocks(k_c, pe_k, w1_k, w2_k)
    vc = compress_blocks(v_c, pe_v, w1_v, w2_v)
    n_cmp = kc.shape[1]
    cmp_lo = jnp.arange(n_cmp) * CMP_STRIDE
    cmp_end = cmp_lo + CMP_BLOCK - 1

    n_sel = S // SEL_BLOCK
    n_top = min(SEL_TOPK, n_sel)
    sel_idx = jnp.arange(n_sel)
    sel_lo = sel_idx * SEL_BLOCK
    overlap = ((cmp_lo[:, None] <= sel_lo[None, :] + SEL_BLOCK - 1)
               & (cmp_end[:, None] >= sel_lo[None, :])).astype(jnp.float32)
    kst = k_s.transpose(0, 2, 1, 3)
    vst = v_s.transpose(0, 2, 1, 3)

    Lw = NSA_WINDOW + Q_BLOCK
    kwp = jnp.pad(k_w, ((0, 0), (NSA_WINDOW, 0), (0, 0), (0, 0)))
    vwp = jnp.pad(v_w, ((0, 0), (NSA_WINDOW, 0), (0, 0), (0, 0)))

    def block(args):
        qblk, gblk, bidx = args
        t = bidx * Q_BLOCK + jnp.arange(Q_BLOCK)
        dist_c = t[:, None] - cmp_end[None, :]
        sc = jnp.einsum('bqgrd,bngd->bgrqn', qblk, kc).astype(jnp.float32) * scale
        p_c = masked_softmax(sc - slopes * dist_c.astype(jnp.float32), dist_c >= 0)
        o_c = jnp.einsum('bgrqn,bngd->bqgrd', p_c.astype(dt), vc)
        imp = jnp.sum(p_c, axis=2) @ overlap
        jt = t // SEL_BLOCK
        valid = sel_lo[None, :] <= t[:, None]
        forced = ((sel_idx[None, :] == 0) | (sel_idx[None, :] == jt[:, None])
                  | (sel_idx[None, :] == jt[:, None] - 1))
        score = jnp.where(valid, jnp.where(forced, SEL_FORCE, imp), -SEL_FORCE)
        _, sel = lax.top_k(score, n_top)
        tok = (sel[..., None] * SEL_BLOCK + jnp.arange(SEL_BLOCK)).reshape(
            B, G, Q_BLOCK, n_top * SEL_BLOCK)
        ks = gather_rows(kst, tok)
        vs = gather_rows(vst, tok)
        dist_s = t[None, None, :, None] - tok
        ss = jnp.einsum('bqgrd,bgqnd->bgrqn', qblk, ks).astype(jnp.float32) * scale
        ss = ss - slopes * dist_s[:, :, None].astype(jnp.float32)
        p_s = masked_softmax(ss, (dist_s >= 0)[:, :, None])
        o_s = jnp.einsum('bgrqn,bgqnd->bqgrd', p_s.astype(dt), vs)
        kw = lax.dynamic_slice_in_dim(kwp, bidx * Q_BLOCK, Lw, axis=1)
        vw = lax.dynamic_slice_in_dim(vwp, bidx * Q_BLOCK, Lw, axis=1)
        key_pos = bidx * Q_BLOCK - NSA_WINDOW + jnp.arange(Lw)
        dist_w = t[:, None] - key_pos[None, :]
        mask_w = (dist_w >= 0) & (dist_w < NSA_WINDOW) & (key_pos >= 0)[None, :]
        sw = jnp.einsum('bqgrd,bkgd->bgrqk', qblk, kw).astype(jnp.float32) * scale
        p_w = masked_softmax(sw - slopes * dist_w.astype(jnp.float32), mask_w)
        o_w = jnp.einsum('bgrqk,bkgd->bqgrd', p_w.astype(dt), vw)
        g = jax.nn.sigmoid(gblk.astype(jnp.float32))
        o = g[..., 0:1] * o_c + g[..., 1:2] * o_s + g[..., 2:3] * o_w
        return o.astype(dt)

    qb = jnp.moveaxis(q.reshape(B, nb, Q_BLOCK, G, R, d), 1, 0)
    gb = jnp.moveaxis(gates.reshape(B, nb, Q_BLOCK, G, R, 3), 1, 0)
    o = lax.map(block, (qb, gb, jnp.arange(nb)))
    return jnp.moveaxis(o, 0, 1).reshape(B, S, G * R * d)

def hybrid_mixer(h, w_in, sinks, pe_k, w1_k, w2_k, pe_v, w1_v, w2_v,
                 w_br_a, w_br_b, w_br_c, w_out):
    B, S, _ = h.shape
    (qa, ka, va, qb, kb, vb, qc, kc, vc, ksl, vsl, kwn, vwn, gc, gates) = split_cols(
        h @ w_in, IN_SPLITS)
    ra = SWA_HEADS // SWA_KV_HEADS
    rc = NSA_HEADS // NSA_KV_HEADS
    kv_a = lambda t: t.reshape(B, S, SWA_KV_HEADS, SWA_HEAD_DIM)
    kv_c = lambda t: t.reshape(B, S, NSA_KV_HEADS, NSA_HEAD_DIM)
    sb = lambda t: t.reshape(B, S, SB_HEADS, SB_HEAD_DIM)
    y_a = swa_attention(qa.reshape(B, S, SWA_KV_HEADS, ra, SWA_HEAD_DIM), kv_a(ka), kv_a(va), sinks)
    y_b = stick_breaking(sb(qb), sb(kb), sb(vb))
    y_c = nsa_attention(qc.reshape(B, S, NSA_KV_HEADS, rc, NSA_HEAD_DIM),
                        gc.reshape(B, S, NSA_KV_HEADS, rc, 3),
                        kv_c(kc), kv_c(vc), kv_c(ksl), kv_c(vsl), kv_c(kwn), kv_c(vwn),
                        pe_k, w1_k, w2_k, pe_v, w1_v, w2_v)
    g_a, g_b, g_c = jnp.split(gates, 3, axis=-1)
    merged = (jax.nn.sigmoid(g_a) * (y_a @ w_br_a)
              + jax.nn.sigmoid(g_b) * (y_b @ w_br_b)
              + jax.nn.sigmoid(g_c) * (y_c @ w_br_c))
    return merged @ w_out

def swiglu(h, w_gate, w_up, w_down):
    return (jax.nn.silu(h @ w_gate) * (h @ w_up)) @ w_down

def setup_inputs(seed: int = 0) -> dict:
    key = jax.random.key(seed)
    ks = jax.random.split(key, 20)
    f32 = jnp.float32

    def nrm(k, shape, fan_in):
        return jax.random.normal(k, shape, f32) * (fan_in ** -0.5)

    def gain(k, shape):
        return 1.0 + 0.02 * jax.random.normal(k, shape, f32)

    cmp_in = CMP_BLOCK * NSA_HEAD_DIM
    w_a = SWA_HEADS * SWA_HEAD_DIM
    w_b = SB_HEADS * SB_HEAD_DIM
    w_c = NSA_HEADS * NSA_HEAD_DIM
    return {
        "x": jax.random.normal(ks[0], (BATCH, SEQ, D_MODEL), f32),
        "norm_mix": gain(ks[1], (DEPTH, D_MODEL)),
        "w_in": nrm(ks[2], (DEPTH, D_MODEL, N_IN), D_MODEL),
        "swa_sinks": 0.5 * jax.random.normal(ks[3], (DEPTH, SWA_HEADS), f32),
        "cmp_pe_k": 0.1 * jax.random.normal(ks[4], (DEPTH, CMP_BLOCK, NSA_HEAD_DIM), f32),
        "cmp_w1_k": nrm(ks[5], (DEPTH, cmp_in, CMP_HIDDEN), cmp_in),
        "cmp_w2_k": nrm(ks[6], (DEPTH, CMP_HIDDEN, NSA_HEAD_DIM), CMP_HIDDEN),
        "cmp_pe_v": 0.1 * jax.random.normal(ks[7], (DEPTH, CMP_BLOCK, NSA_HEAD_DIM), f32),
        "cmp_w1_v": nrm(ks[8], (DEPTH, cmp_in, CMP_HIDDEN), cmp_in),
        "cmp_w2_v": nrm(ks[9], (DEPTH, CMP_HIDDEN, NSA_HEAD_DIM), CMP_HIDDEN),
        "w_branch_swa": nrm(ks[10], (DEPTH, w_a, D_MODEL), w_a),
        "w_branch_sb": nrm(ks[11], (DEPTH, w_b, D_MODEL), w_b),
        "w_branch_nsa": nrm(ks[12], (DEPTH, w_c, D_MODEL), w_c),
        "w_out": nrm(ks[13], (DEPTH, D_MODEL, D_MODEL), D_MODEL),
        "norm_ffn": gain(ks[14], (DEPTH, D_MODEL)),
        "w_gate": nrm(ks[15], (DEPTH, D_MODEL, D_FF), D_MODEL),
        "w_up": nrm(ks[16], (DEPTH, D_MODEL, D_FF), D_MODEL),
        "w_down": nrm(ks[17], (DEPTH, D_FF, D_MODEL), D_FF),
        "norm_final": gain(ks[18], (D_MODEL,)),
    }

def reference(x, norm_mix, w_in, swa_sinks, cmp_pe_k, cmp_w1_k, cmp_w2_k,
              cmp_pe_v, cmp_w1_v, cmp_w2_v, w_branch_swa, w_branch_sb, w_branch_nsa,
              w_out, norm_ffn, w_gate, w_up, w_down, norm_final):
    for layer in range(DEPTH):
        h = rms_norm(x, norm_mix[layer])
        x = x + hybrid_mixer(h, w_in[layer], swa_sinks[layer],
                             cmp_pe_k[layer], cmp_w1_k[layer], cmp_w2_k[layer],
                             cmp_pe_v[layer], cmp_w1_v[layer], cmp_w2_v[layer],
                             w_branch_swa[layer], w_branch_sb[layer], w_branch_nsa[layer],
                             w_out[layer])
        h = rms_norm(x, norm_ffn[layer])
        x = x + swiglu(h, w_gate[layer], w_up[layer], w_down[layer])
    return rms_norm(x, norm_final)


_drawn_inputs = setup_inputs


def setup_inputs(seed=0):
    import zlib

    import numpy as np

    out = dict(_drawn_inputs(seed))
    spreads = {}
    factors = {'norm_mix': 4.566,
     'swa_sinks': 21.219,
     'cmp_pe_k': 8.0,
     'cmp_pe_v': 2.958,
     'norm_ffn': 4.038,
     'norm_final': 8.078}
    for name, (base, spread) in spreads.items():
        noise = np.random.default_rng([zlib.crc32(name.encode()), seed]).standard_normal(out[name].shape)
        drawn = base * np.exp(spread * noise) if base else spread * noise
        out[name] = jnp.asarray(drawn.astype(out[name].dtype))
    for name, factor in factors.items():
        out[name] = (out[name] * factor).astype(out[name].dtype)
    return out
```

```python
from contextlib import ExitStack

import concourse.bass as bass
from concourse import mybir

F32 = mybir.dt.float32
F32R = mybir.dt.float32r
ALU = mybir.AluOpType
ACT = mybir.ActivationFunctionType
AX_X = mybir.AxisListType.X

P = 128
TT = 2
S = TT * P
D = 2048
KD = D // P
W = 512
NC_D = D // W
FF = 5632
KF = FF // P
NC_F = FF // W
HD = 64
HEADS = 8
PAIRS = HEADS // 2
SB_HEADS = 4
N_CMP = 15
NP_CMP = 16
MLP_W = 256
EPS = 1e-6
NEG = -1.0e35
SCALE = 0.125
SB_SCALE = float(128) ** -0.5

QA, KA, VA = 0, 512, 640
QB, KB, VB = 768, 1280, 1792
QC, KCMP, VCMP, KSEL, VSEL, KWIN, VWIN = 2304, 2816, 2944, 3072, 3200, 3328, 3456
GC, NGC = 3584, 24
N_PROJ = 3584
GATES = 3608

UK = 2
RING = 4
UPC = KD // UK
N_QKV = N_PROJ // W
U_GC = N_QKV * UPC
U_MIX = U_GC + 1
U_OUT = U_MIX + 12 * UPC + 12 * 2
U_FFN = U_OUT + NC_D * UPC
U_DOWN = U_FFN + 2 * NC_F * UPC
UPD = KF // UK
U_END = U_DOWN + NC_D * UPD
LAG = 3
SIG = 6

GATE_COL = [GATES + 2 * D, GATES, GATES + D]


def mix_plan():
    plan, u = [], U_MIX
    for g in range(12):
        plan.append(("gate", g, u))
        u += UPC
        if g >= 5:
            plan.append(("branch", g - 5, u))
            u += 2
    for b in range(7, 12):
        plan.append(("branch", b, u))
        u += 2
    assert u == U_OUT
    return plan


MIX = mix_plan()
CHUNKS = [("qkv", c, c * UPC, UPC) for c in range(N_QKV)] + [("gc", 0, U_GC, 1)]
CHUNKS += [(k, i, u, UPC if k == "gate" else 2) for k, i, u in MIX]
CHUNKS += [("out", c, U_OUT + c * UPC, UPC) for c in range(NC_D)]
Q_FFN = len(CHUNKS)
Q_DOWN = Q_FFN + 2 * NC_F
CHUNK_OF = {}
for _q, (_k, _i, _u, _n) in enumerate(CHUNKS):
    for _j in range(_n):
        CHUNK_OF[_u + _j] = (_q, _j)
BRANCH_END = {i: u + 1 for k, i, u in MIX if k == "branch"}

CMP = 8
N_SOFT = 13


def soft(i):
    if i < CMP:
        return ("sel", "win")[i % 2], i // 2
    return ("cmp", None) if i == CMP else ("swa", i - CMP - 1)


def soft_slot(i):
    return 10 + 3 * i if i <= CMP else 15 + 3 * i


SOFT_AT = {soft_slot(i): i for i in range(N_SOFT)}
PROBS_T_AT = {soft_slot(i) + 4: i for i in range(N_SOFT)}
VALUES_AT = {soft_slot(i) + 6: i for i in range(N_SOFT)}
PREP = [(0, "q", QC, 0), (1, "q", QC, 1), (2, "k", KSEL, 0), (3, "k", KWIN, 1), (4, "c", KCMP, 0), (5, "c", VCMP, 1),
        (36, "q", QA, 0), (37, "q", QA, 1), (39, "k", KA, 0),
        (54, "sq", QB, 0), (55, "sq", QB, 1), (57, "sk", KB, 0), (58, "sk", KB, 1)]
PREP_AT = {p[0]: n for n, p in enumerate(PREP)}
MLP_SLOTS = {7: "up_k", 10: "down_k", 11: "up_v", 13: "down_v"}


def stick_slot(h, step):
    return 76 + 6 * h + step


STICK = {}
for _h in range(SB_HEADS):
    for _s in (0, 4, 8):
        STICK.setdefault(stick_slot(_h, _s), []).append((_h, _s))


def merge_T_at(m):
    return BRANCH_END[2 * NC_D + m] + LAG


def out_T_at(m):
    return U_OUT + (m + 1) * UPC - 1 + LAG


def evac_engine(q):
    if q < Q_FFN:
        return "act" if CHUNKS[q][0] in ("gate", "gc") else "dve"
    return ("act", "up")[(q - Q_FFN) % 2] if q < Q_DOWN else "dve"


def evac_count(q):
    return sum(evac_engine(r) == evac_engine(q) for r in range(q + 1))


def slope(h):
    return 2.0 ** -(h + 1)


def build_layer(nc, x_in, norm_mix, w_in, sinks, pe_k, w1_k, w2_k, pe_v, w1_v, w2_v,
                w_br_a, w_br_b, w_br_c, w_out, norm_ffn, w_gate, w_up, w_down, norm_final, out):
    ctx = ExitStack()
    with ctx:
        top = [(nc.sbuf_base + 31) // 32 * 32]

        def at(name, shape, offset, dt=F32):
            return nc.alloc_sbuf_tensor_at(name, [P] + shape, dt, offset=offset)

        def place(name, shape, dt=F32):
            n = 4
            for s in shape:
                n *= s
            n = (n + 31) // 32 * 32
            t = at(name, shape, top[0], dt)
            top[0] += n
            assert top[0] <= nc.sbuf_top, name
            return t

        raw = place("raw_ring", [RING, UK, W])
        whi = place("weight_hi_ring", [RING, UK, W], F32R)
        wlo = place("weight_lo_ring", [RING, UK, W], F32R)
        ident = place("identity", [P])
        gainT = place("gains_T", [4, KD])
        sumsq = place("sumsq", [TT, NC_D])
        stat = place("stat", [6, TT])
        rstd = place("rstd", [TT])
        X = place("x", [TT, D])

        low = top[0]
        hT_hi = place("hT_hi", [KD, S], F32R)
        hT_lo = place("hT_lo", [KD, S], F32R)
        proj = place("proj", [TT, N_PROJ])
        sig = place("sigmoid_gates", [SIG, TT, W])
        sc = place("scores", [2, 2, 3 * P])
        pT = place("probs_T", [2, 2, 3 * P])
        mid = top[0]
        merged = place("merged", [TT, D])
        yT_hi = place("yT_hi", [2, 4, S], F32R)
        yT_lo = place("yT_lo", [2, 4, S], F32R)
        negdist = place("negdist", [S])
        negdist_w = place("negdist_window", [S])
        bias_c = place("bias_compressed", [TT, HEADS, NP_CMP])
        nd_c = place("negdist_compressed", [TT, NP_CMP])
        valid_c = place("valid_compressed", [TT, NP_CMP])
        kcz = place("kc_zero_padded", [2, 2, NP_CMP])
        hid_k = place("hidden_k", [2, 2, NP_CMP])
        hid_v = place("hidden_v", [2, 2, 4, NP_CMP])
        w2k = place("w2_k_twice", [2, 2, HD])
        w2v = place("w2_v", [2, HD])
        vz = place("vc_block_diagonal", [HEADS, HD])
        head_mask = place("head_mask", [HEADS])
        gsig = place("nsa_gates", [TT, NGC])
        sinkb = place("sinks", [HEADS])
        small = place("softmax_small", [2, 6, 2, 2])
        csum = place("cmp_small", [3, TT, HEADS])
        strict = place("strict_mask", [3 * P])
        later = place("later", [P])
        ones = place("ones", [P])

        h2T_hi = at("h2T_hi", [KD, S], mid, F32R)
        h2T_lo = at("h2T_lo", [KD, S], mid + 4 * KD * S, F32R)
        actT_hi = at("actT_hi", [KF, S], low, F32R)
        actT_lo = at("actT_lo", [KF, S], low + 4 * KF * S, F32R)
        silu = at("silu", [TT, W], low + 8 * KF * S)
        act_rows = at("act_rows", [TT, W], low + 8 * KF * S + 4 * TT * W)
        assert low + 8 * KF * S + 8 * TT * W <= mid
        gfin = at("norm_final", [D], mid)

        xs = X[:, :, :].rearrange("p t d -> p (t d)")
        qT = xs[:, 0:1024].rearrange("p (r s) -> p r s", r=PAIRS)
        kz = [xs[:, 1024 * (1 + n):1024 * (2 + n)].rearrange("p (g a s) -> p g a s", g=2, a=2) for n in range(2)]
        blkT = [xs[:, 3072 + 512 * n:3584 + 512 * n].rearrange("p (k c) -> p k c", k=KD) for n in range(2)]
        sqT = xs[:, 2048:3072].rearrange("p (h s) -> p h s", h=SB_HEADS)
        skT = xs[:, 3072:4096].rearrange("p (h s) -> p h s", h=SB_HEADS)
        rows = sig[:, 0, 0, :].rearrange("p (a c) -> p a c", a=4)
        yacc = merged[:, 0, 0:PAIRS * S].rearrange("p (r s) -> p r s", r=PAIRS)
        w1 = merged[:, :, :].rearrange("p t d -> p (t d)").rearrange("p (k m) -> p k m", k=KD)
        s_z = sc[:, 0, 1, :]
        s_ln = sc[:, 1, 0, :]
        s_sp = sc[:, 1, 1, :]
        s_arg = pT[:, 0, 0, :]
        s_surv = pT[:, 0, 1, :]
        s_w = pT[:, 1, 0, :]

        bank = [ctx.enter_context(nc.psum_tensor(f"bank{i}", [P, W], F32)) for i in range(8)]

        def sem(name):
            return ctx.enter_context(nc.semaphore(name))

        raw_ready = [sem(f"raw_ready{i}") for i in range(RING)]
        hi_ready = sem("hi_ready")
        lo_ready = sem("lo_ready")
        unit_used = sem("unit_used")
        emptied = {"act": sem("emptied_by_act"), "dve": sem("emptied_by_dve")}
        x_ready = [sem(f"x_ready{i}") for i in range(NC_D)]
        rows_ready = sem("rows_ready")
        ident_ready = sem("ident_ready")
        gains_full = sem("gains_full")
        gains_ready = sem("gains_ready")
        t_full = sem("transposes_full")
        t_hi = sem("transposed_hi")
        t_lo = sem("transposed_lo")
        squares = sem("squares")
        mean_ready = sem("mean_ready")
        root_ready = sem("root_ready")
        rstd_ready = sem("rstd_ready")
        x_again = sem("x_again")
        consts_ready = sem("consts_ready")
        zeros_ready = sem("zeros_ready")
        w1_ready = sem("w1_ready")
        w2_ready = sem("w2_ready")
        sinks_ready = sem("sinks_ready")
        prep_full = sem("prep_full")
        prep_done = sem("prep_done")
        nsa_gates = sem("nsa_gates_ready")
        mlp_up = sem("mlp_up")
        hid_ready = sem("hidden_ready")
        mlp_down = sem("mlp_down")
        cmp_ready = sem("compressed_ready")
        scores_full = sem("scores_full")
        scores_sb = sem("scores_masked")
        sink_exp_in = sem("sink_exp_in")
        exps = sem("exps")
        probs = sem("probs")
        probsT_full = sem("probsT_full")
        probsT = sem("probsT")
        values_full = sem("values_full")
        values_read = sem("values_read")
        z_full = sem("stick_z_full")
        z_ready = sem("stick_z_ready")
        z_ln = sem("stick_ln")
        z_sp = sem("stick_softplus")
        z_spm = sem("stick_softplus_masked")
        z_cum = sem("stick_cum_full")
        z_arg = sem("stick_arg")
        z_surv = sem("stick_surv")
        z_w = sem("stick_weights")
        z_val = sem("stick_values_full")
        act_full = sem("act_rows_ready")
        silu_ready = sem("silu_ready")
        aT_full = sem("actT_full")
        aT_hi = sem("actT_hi_ready")
        aT_lo = sem("actT_ready")
        gfin_ready = sem("gfin_ready")
        gained = sem("gained")
        result = [sem(f"result_tile{t}") for t in range(TT)]
        stored = sem("stored")
        dve_step = sem("dve_step")
        act_step = sem("act_step")
        pool_step = sem("pool_step")
        steps = {"dve": 0, "act": 0, "pool": 0}
        step_sem = {"dve": dve_step, "act": act_step, "pool": pool_step}

        def link(eng, name, ins):
            steps[name] += 1
            ins.then_inc(step_sem[name], 1)
            eng.wait_ge(step_sem[name], steps[name])

        def blocks(w):
            return w.rearrange("(k p) n -> p k n", p=P)

        win_b, wout_b, wg_b, wu_b, wd_b = (blocks(w) for w in (w_in, w_out, w_gate, w_up, w_down))
        br_b = [blocks(w) for w in (w_br_c, w_br_a, w_br_b)]
        x_b = x_in.rearrange("(t p) d -> p t d", p=P)
        out_b = out.rearrange("(t p) d -> p t d", p=P)

        branch_q = {CHUNKS[q][1]: q for q in range(Q_FFN) if CHUNKS[q][0] == "branch"}
        gate_q = {CHUNKS[q][1]: q for q in range(Q_FFN) if CHUNKS[q][0] == "gate"}
        out_q = {CHUNKS[q][1]: q for q in range(Q_FFN) if CHUNKS[q][0] == "out"}

        block = ctx.enter_context(nc.Block())

        @block.sync
        def _(sp):
            def load(u, slot, src, more=0):
                sp.dma_start(raw[:, slot, :, :], src).then_inc(raw_ready[slot], 16)

            def free(count):
                sp.wait_ge(lo_ready, count)

            def straight(u):
                q, j = CHUNK_OF[u]
                kind, i, _, _ = CHUNKS[q]
                if u >= RING:
                    free(u - RING + 1)
                if kind == "gc":
                    sp.dma_start(raw[:, u % RING, :, :].rearrange("p k w -> p (k w)")[:, 0:KD * NGC]
                                 .rearrange("p (k w) -> p k w", k=KD),
                                 win_b[:, :, GC:GC + NGC]).then_inc(raw_ready[u % RING], 16)
                    return
                ks = slice(UK * j, UK * j + UK)
                if kind == "qkv":
                    src = win_b[:, ks, i * W:(i + 1) * W]
                elif kind == "gate":
                    c = GATE_COL[i // NC_D] + (i % NC_D) * W
                    src = win_b[:, ks, c:c + W]
                elif kind == "branch":
                    c = (i % NC_D) * W
                    src = br_b[i // NC_D][:, ks, c:c + W]
                else:
                    src = wout_b[:, ks, i * W:(i + 1) * W]
                load(u, u % RING, src)

            def xload(c):
                sp.dma_start(X[:, :, c * W:(c + 1) * W], x_b[:, :, c * W:(c + 1) * W]).then_inc(x_ready[c], 16)

            xload(0)
            straight(0)
            xload(1)
            straight(1)
            xload(2)
            xload(3)
            for u in range(2, UPC):
                straight(u)
            with sp.Fori(0, (N_QKV - 1) // 2) as i:
                for c in range(2):
                    for j in range(UPC):
                        u0 = UPC + c * UPC + j
                        sp.wait_ge(lo_ready, i * (2 * UPC) + (u0 - RING + 1))
                        load(u0, u0 % RING, win_b[:, UK * j:UK * j + UK, bass.ts(i * 2 + (1 + c), W)])
            for u in range(U_GC, U_FFN):
                straight(u)
            with sp.Fori(0, NC_F) as i:
                for c, w in enumerate((wg_b, wu_b)):
                    for j in range(UPC):
                        u0 = U_FFN + c * UPC + j
                        sp.wait_ge(lo_ready, i * (2 * UPC) + (u0 - RING + 1))
                        load(u0, u0 % RING, w[:, UK * j:UK * j + UK, bass.ts(i, W)])
            with sp.Fori(0, NC_D // 2) as i:
                for c in range(2):
                    for j in range(UPD):
                        u0 = U_DOWN + c * UPD + j
                        sp.wait_ge(lo_ready, i * (2 * UPD) + (u0 - RING + 1))
                        load(u0, u0 % RING, wd_b[:, UK * j:UK * j + UK, bass.ts(i * 2 + c, W)])
            for n in range(4):
                for t in range(TT):
                    sp.wait_ge(result[t], n + 1)
                sp.dma_start(out_b[:, :, n * W:(n + 1) * W], X[:, :, n * W:(n + 1) * W]).then_inc(stored, 16)
            sp.wait_ge(stored, 64)

        @block.gpsimd
        def _(pool):
            pool.dma_start(rows[0:KD, 0, :], norm_mix.rearrange("(k p) -> k p", p=P)).then_inc(rows_ready, 16)
            pool.dma_start(rows[0:KD, 1, :], norm_ffn.rearrange("(k p) -> k p", p=P)).then_inc(rows_ready, 16)
            pool.dma_start(rows[0:KD, 2, :], pe_k.rearrange("(k a) d -> k (a d)", a=2)).then_inc(rows_ready, 16)
            pool.dma_start(rows[0:KD, 3, :], pe_v.rearrange("(k a) d -> k (a d)", a=2)).then_inc(rows_ready, 16)

            def select(t, pattern, base, cm, op, fill):
                return pool.affine_select(out=t, in_=t, compare_op=op, fill=fill, base=base,
                                          pattern=pattern, channel_multiplier=cm)

            link(pool, "pool", pool.memset(ident[:, :], 0.0))
            select(ident[:, :], [[-1, P]], 0, 1, ALU.not_equal, 1.0).then_inc(ident_ready, 1)
            pool.iota(negdist[:, :], pattern=[[1, S]], base=-P, channel_multiplier=-1,
                      allow_small_or_imprecise_dtypes=True)
            link(pool, "pool", pool.iota(nd_c[:, :, :], pattern=[[-P, TT], [NP_CMP, NP_CMP]], base=31,
                                         channel_multiplier=-1, allow_small_or_imprecise_dtypes=True))
            select(nd_c[:, :, :], [[P, TT], [-NP_CMP, NP_CMP]], -31, 1, ALU.is_ge, NEG)
            link(pool, "pool", select(negdist[:, :], [[-1, S]], P, 1, ALU.is_ge, NEG))
            pool.affine_select(out=negdist_w[:, :], in_=negdist[:, :], compare_op=ALU.is_ge, fill=NEG, base=-1,
                               pattern=[[1, S]], channel_multiplier=-1)
            for h in range(HEADS):
                pool.tensor_scalar(bias_c[:, :, h, :], nd_c[:, :, :], slope(h), None, ALU.mult)
            pool.memset(valid_c[:, :, :], 1.0)
            pool.memset(strict[:, :], 1.0)
            pool.memset(later[:, :], 1.0)
            pool.memset(ones[:, :], 1.0)
            pool.memset(kcz[:, :, :, :], 0.0)
            link(pool, "pool", pool.memset(head_mask[:, :], 1.0))
            select(valid_c[:, :, :], [[P, TT], [-NP_CMP, NP_CMP]], -31, 1, ALU.is_ge, 0.0)
            select(strict[:, 0:P], [[1, P]], 0, -1, ALU.is_gt, 0.0)
            select(strict[:, 2 * P:3 * P], [[1, P]], 0, -1, ALU.is_gt, 0.0)
            select(later[:, :], [[-1, P]], 0, 1, ALU.is_gt, 0.0)
            link(pool, "pool", select(head_mask[:, :], [[-NP_CMP, HEADS]], 0, 1, ALU.is_ge, 0.0))
            select(head_mask[:, :], [[NP_CMP, HEADS]], NP_CMP - 1, -1, ALU.is_ge, 0.0).then_inc(consts_ready, 1)

            pool.dma_start(w1[:, :, :], w1_k.rearrange("(k p) m -> p k m", p=P)).then_inc(w1_ready, 16)
            w2k_src = w2_k.rearrange("(k p) d -> p k d", p=P)
            pool.dma_start(w2k[:, :, 0, :], w2k_src).then_inc(w2_ready, 16)
            pool.dma_start(w2k[:, :, 1, :], w2k_src).then_inc(w2_ready, 16)
            pool.dma_start(w2v[:, :, :], w2_v.rearrange("(k p) d -> p k d", p=P)).then_inc(w2_ready, 16)
            pool.dma_start(sinkb[:, :], sinks.partition_broadcast(P)).then_inc(sinks_ready, 16)

            pool.wait_ge(t_lo, UPC)
            pool.wait_ge(squares, 2 * NC_D)
            pool.memset(xs[:, 1024:3072], 0.0)
            pool.memset(xs[:, 3072:4096], 0.0).then_inc(zeros_ready, 1)
            pool.wait_ge(mlp_up, 1)
            pool.dma_start(w1[:, :, :], w1_v.rearrange("(k p) m -> p k m", p=P)).then_inc(w1_ready, 16)

            for h in range(SB_HEADS):
                pool.wait_ge(z_sp, h + 1)
                pool.tensor_tensor(s_sp, s_sp, strict[:, :], ALU.mult).then_inc(z_spm, 1)
                pool.wait_ge(z_surv, h + 1)
                if h >= 1:
                    pool.wait_ge(z_val, h)
                pool.tensor_tensor(s_w, s_surv, strict[:, :], ALU.mult).then_inc(z_w, 1)
                if h == SB_HEADS - 1:
                    pool.dma_start(X[:, :, :], x_b).then_inc(x_again, 16)

            pool.wait_ge(unit_used, U_DOWN)
            pool.dma_start(gfin[:, :], norm_final.partition_broadcast(P)).then_inc(gfin_ready, 16)
            pool.wait_ge(gfin_ready, 16)
            for n in range(NC_D):
                pool.wait_ge(squares, 2 * NC_D * 2 + 2 * (n + 1))
                for t in range(TT):
                    last = pool.tensor_tensor(X[:, t, n * W:(n + 1) * W], X[:, t, n * W:(n + 1) * W],
                                              gfin[:, n * W:(n + 1) * W], ALU.mult)
                last.then_inc(gained, 1)

        @block.tensor
        def _(pe):
            def transpose(dst, src, n=P):
                return pe.transpose(dst, src, ident[0:n, 0:n])

            def products(slot, j, lhs, pair, first, last, k0):
                l_hi, l_lo = lhs
                for k in range(UK):
                    for t in range(TT):
                        dst = bank[2 * pair + t][:, :]
                        x_hi, x_lo = (m[:, k0 + k, t * P:(t + 1) * P] for m in (l_hi, l_lo))
                        pe.matmul(dst, x_hi, whi[:, slot, k, :], start=first and k == 0, stop=False)
                        pe.matmul(dst, x_hi, wlo[:, slot, k, :], start=False, stop=False)
                        m = pe.matmul(dst, x_lo, whi[:, slot, k, :], start=False, stop=last and k == UK - 1)
                return m

            def unit(u, lhs, q, j, n, k0=None):
                pe.wait_ge(lo_ready, u + 1)
                m = products(u % RING, j, lhs, q % 2, j == 0, j == n - 1, UK * j if k0 is None else k0)
                m.then_inc(unit_used, 1)

            def pair_free(q):
                if q >= 2:
                    pe.wait_ge(emptied[evac_engine(q - 2)], evac_count(q - 2))

            def straight(u):
                q, j = CHUNK_OF[u]
                kind, i, _, n = CHUNKS[q]
                if j == 0:
                    pair_free(q)
                    if q == 1:
                        pe.wait_ge(squares, 2 * NC_D)
                if kind == "gc":
                    pe.wait_ge(lo_ready, u + 1)
                    h_, l_ = (w[:, u % RING, :, :].rearrange("p k w -> p (k w)") for w in (whi, wlo))
                    for k in range(KD):
                        for t in range(TT):
                            dst = bank[2 * (q % 2) + t][:, 0:NGC]
                            x_hi, x_lo = (m[:, k, t * P:(t + 1) * P] for m in (hT_hi, hT_lo))
                            cols = slice(k * NGC, (k + 1) * NGC)
                            pe.matmul(dst, x_hi, h_[:, cols], start=k == 0, stop=False)
                            pe.matmul(dst, x_hi, l_[:, cols], start=False, stop=False)
                            m = pe.matmul(dst, x_lo, h_[:, cols], start=False, stop=k == KD - 1)
                    m.then_inc(unit_used, 1)
                    return
                if kind == "branch":
                    s = i // NC_D
                    pe.wait_ge(values_read, (CMP + 1, N_SOFT, N_SOFT + SB_HEADS)[s])
                    lhs = (yT_hi[:, s % 2, :, :], yT_lo[:, s % 2, :, :])
                elif kind == "out":
                    lhs = (hT_hi, hT_lo)
                    if i == 0:
                        pe.wait_ge(t_lo, UPC + j + 1)
                else:
                    lhs = (hT_hi, hT_lo)
                    if q == 0:
                        pe.wait_ge(t_lo, j + 1)
                unit(u, lhs, q, j, n)

            def transposes_of_rows(n, b, src):
                for k in range(UK):
                    for t in range(TT):
                        m = transpose(bank[b][:, k * S + t * P:k * S + (t + 1) * P], src[:, t, k * P:(k + 1) * P])
                m.then_inc(t_full, 1)

            def values(i, h, v):
                dst = bank[7][HD * h:HD * (h + 1), :]
                pe.matmul(dst[:, S:2 * S], v[0], pT[:, i % 2, h, 0:S], start=True, stop=False)
                return pe.matmul(dst[:, S + P:2 * S], v[1], pT[:, i % 2, h, S:3 * P], start=False, stop=True)

            def mixer_step(k):
                if k in PREP_AT:
                    p = PREP_AT[k]
                    _, what, col, b = PREP[p]
                    if p == 0:
                        pe.wait_ge(emptied["dve"], N_QKV)
                    if p >= 2:
                        pe.wait_ge(prep_done, p - 1)
                    if p == 6:
                        pe.wait_ge(scores_sb, CMP + 1)
                    if p == 9:
                        pe.wait_ge(scores_sb, N_SOFT)
                    dst = bank[4 + b]
                    if what in ("q", "sq", "sk"):
                        for a in range(2):
                            for t in range(TT):
                                c = col + P * (2 * b + a)
                                m = transpose(dst[:, a * S + t * P:a * S + (t + 1) * P], proj[:, t, c:c + P])
                    else:
                        for g in range(2):
                            for t in range(TT):
                                for a in range(2):
                                    m = pe.matmul(dst[HD * a:HD * (a + 1), g * S + t * P:g * S + (t + 1) * P],
                                                  proj[:, t, col + HD * g:col + HD * (g + 1)], ident[:, :],
                                                  start=True, stop=True)
                    m.then_inc(prep_full, 1)
                mlp = MLP_SLOTS.get(k)
                if mlp in ("up_k", "up_v"):
                    n = 0 if mlp == "up_k" else 1
                    pe.wait_ge(w1_ready, 16 * (n + 1))
                    pe.wait_ge(prep_done, 5 + n)
                    for a in range(2):
                        for kt in range(KD):
                            m = pe.matmul(bank[6 + n][:, 32 * a:32 * (a + 1)], w1[:, kt, P * a:P * (a + 1)],
                                          blkT[n][:, kt, :], start=kt == 0, stop=kt == KD - 1)
                    m.then_inc(mlp_up, 1)
                if mlp == "down_k":
                    pe.wait_ge(w2_ready, 48)
                    pe.wait_ge(hid_ready, 1)
                    for a in range(2):
                        m = pe.matmul(bank[6][:, 0:32], w2k[:, a, :, :].rearrange("p r d -> p (r d)"),
                                      hid_k[:, a, :, :].rearrange("p g n -> p (g n)"), start=a == 0, stop=a == 1)
                    m.then_inc(mlp_down, 1)
                if mlp == "down_v":
                    pe.wait_ge(hid_ready, 2)
                    for a in range(2):
                        m = pe.matmul(bank[7][:, 0:HD], hid_v[:, a, :, :, :].rearrange("p g r n -> p (g r n)"),
                                      w2v[:, a, :], start=a == 0, stop=a == 1)
                    m.then_inc(mlp_down, 1)
                if k in SOFT_AT:
                    i = SOFT_AT[k]
                    kind, pr = soft(i)
                    pe.wait_ge(prep_done, 6 if i <= CMP else 9)
                    if i >= 1:
                        pe.wait_ge(scores_sb, i)
                    if kind == "cmp":
                        pe.wait_ge(cmp_ready, 1)
                        for pr in range(PAIRS):
                            for t in range(TT):
                                m = pe.matmul(bank[4][:, t * P + 32 * pr:t * P + 32 * (pr + 1)],
                                              qT[:, pr, t * P:(t + 1) * P],
                                              kcz[:, pr // 2, :, :].rearrange("p a n -> p (a n)"),
                                              start=True, stop=True)
                    else:
                        keys = kz[1 if kind == "win" else 0][:, pr // 2, :, :]
                        pe.matmul(bank[5][:, 0:S], qT[:, pr, 0:P], keys[:, :, 0:P], start=True, stop=True)
                        m = pe.matmul(bank[4][:, :], qT[:, pr, P:S], keys, start=True, stop=True)
                    m.then_inc(scores_full, 1)
                if k in PROBS_T_AT:
                    i = PROBS_T_AT[k]
                    pe.wait_ge(probs, i + 1)
                    pe.wait_ge(cmp_ready, 2)
                    if i >= 1:
                        pe.wait_ge(values_read, i)
                    if soft(i)[0] == "cmp":
                        for t in range(TT):
                            m = transpose(bank[6][:, t * P:(t + 1) * P], sc[:, i % 2, 0, t * P:(t + 1) * P])
                    else:
                        for h in range(2):
                            transpose(bank[7][:, h * P:(h + 1) * P], sc[:, i % 2, h, 0:P])
                            for n in range(2):
                                m = transpose(bank[6][:, (2 * h + n) * P:(2 * h + n + 1) * P],
                                              sc[:, i % 2, h, (1 + n) * P:(2 + n) * P])
                    m.then_inc(probsT_full, 1)
                if k in VALUES_AT:
                    i = VALUES_AT[k]
                    kind, pr = soft(i)
                    pe.wait_ge(probsT, i + 1)
                    if kind == "cmp":
                        for pr in range(PAIRS):
                            m = pe.matmul(bank[7 - pr // 2][:, (pr % 2) * S:(pr % 2 + 1) * S],
                                          vz[:, 2 * pr:2 * pr + 2, :].rearrange("p h d -> p (h d)"),
                                          pT[:, i % 2, 0, 0:S], start=True, stop=True)
                    else:
                        c = {"sel": VSEL, "win": VWIN, "swa": VA}[kind] + HD * (pr // 2)
                        for h in range(2):
                            m = values(i, h, [proj[:, t, c:c + HD] for t in range(TT)])
                    m.then_inc(values_full, 1)
                for h, s in STICK.get(k, []):
                    if s == 0:
                        pe.wait_ge(prep_done, len(PREP))
                        if h >= 2:
                            pe.wait_ge(z_ready, h - 1)
                        dst = bank[4 + h % 2]
                        pe.matmul(dst[:, 0:S], skT[:, h, 0:P], sqT[:, h, :], start=True, stop=True)
                        pe.matmul(dst[:, S:3 * P], skT[:, h, P:S], sqT[:, h, P:S], start=True,
                                  stop=True).then_inc(z_full, 1)
                    if s == 4:
                        pe.wait_ge(z_spm, h + 1)
                        pe.wait_ge(consts_ready, 1)
                        if h >= 1:
                            pe.wait_ge(z_arg, h)
                        pe.matmul(bank[6][:, 0:3 * P], later[:, :], s_sp, start=True, stop=False)
                        pe.matmul(bank[6][:, P:S], ones[:, :], s_sp[:, S:3 * P], start=False,
                                  stop=True).then_inc(z_cum, 1)
                    if s == 8:
                        pe.wait_ge(z_w, h + 1)
                        pe.wait_ge(values_read, N_SOFT + h)
                        pe.matmul(bank[7][:, 0:S], proj[:, 0, VB + P * h:VB + P * (h + 1)], s_w[:, 0:S],
                                  start=True, stop=False)
                        pe.matmul(bank[7][:, P:S], proj[:, 1, VB + P * h:VB + P * (h + 1)], s_w[:, S:3 * P],
                                  start=False, stop=True).then_inc(z_val, 1)

            def follow(u):
                mixer_step(u - U_MIX)
                for m in range(NC_D):
                    if u == merge_T_at(m):
                        pe.wait_ge(emptied["dve"], evac_count(branch_q[2 * NC_D + m]))
                        for g in range(2):
                            n = UPC + 2 * m + g
                            if n >= UPC + 2:
                                pe.wait_ge(t_lo, n - 1)
                            else:
                                pe.wait_ge(z_ready, SB_HEADS)
                            transposes_of_rows(n, 4 + g, merged[:, :, (4 * m + 2 * g) * P:(4 * m + 2 * g + 2) * P])
                    if u == out_T_at(m):
                        pe.wait_ge(emptied["dve"], evac_count(out_q[m]))
                        for g in range(2):
                            n = 2 * UPC + 2 * m + g
                            pe.wait_ge(t_lo, n - 1)
                            transposes_of_rows(n, 4 + g, X[:, :, (4 * m + 2 * g) * P:(4 * m + 2 * g + 2) * P])

            def act_transposes(count):
                pe.wait_ge(act_full, count)
                for g in range(2):
                    for k in range(UK):
                        for t in range(TT):
                            m = transpose(bank[4 + g][:, k * S + t * P:k * S + (t + 1) * P],
                                          act_rows[:, t, (2 * g + k) * P:(2 * g + k + 1) * P])
                    m.then_inc(aT_full, 1)

            pe.wait_ge(ident_ready, 1)
            pe.wait_ge(rows_ready, 64)
            for a in range(4):
                m = transpose(bank[2][:, KD * a:KD * (a + 1)], rows[0:KD, a, :], KD)
            m.then_inc(gains_full, 1)

            def x_transposes(m):
                pe.wait_ge(x_ready[m // 2], 16)
                if m >= 4:
                    pe.wait_ge(t_lo, m - 3)
                transposes_of_rows(m, 4 + m % 4, X[:, :, 2 * m * P:(2 * m + 2) * P])

            for m in range(4):
                x_transposes(m)
            for u in range(UPC):
                straight(u)
                if u + 4 < UPC:
                    x_transposes(u + 4)
            with pe.Fori(0, (N_QKV - 1) // 2) as i:
                for c in range(2):
                    q0 = 1 + c
                    if c == 0:
                        pe.wait_ge(squares, 2 * NC_D)
                    for j in range(UPC):
                        u0 = UPC * q0 + j
                        pe.wait_ge(lo_ready, i * (2 * UPC) + (u0 + 1))
                        products(u0 % RING, j, (hT_hi, hT_lo), q0 % 2, j == 0, j == UPC - 1,
                                 UK * j).then_inc(unit_used, 1)
            for u in range(U_GC, U_FFN):
                straight(u)
                follow(u)
            for c in range(2):
                q = Q_FFN + c
                pair_free(q)
                for j in range(UPC):
                    u = U_FFN + c * UPC + j
                    if c == 0:
                        pe.wait_ge(t_lo, 2 * UPC + j + 1)
                    unit(u, (h2T_hi, h2T_lo), q, j, UPC)
                    if u == out_T_at(NC_D - 1):
                        follow(u)
            with pe.Fori(1, NC_F) as i:
                for c in range(2):
                    if c == 0:
                        pe.wait_ge(emptied["act"], i + (evac_count(Q_FFN) - 1))
                    else:
                        pe.wait_ge(act_full, i)
                    for j in range(UPC):
                        u0 = U_FFN + c * UPC + j
                        pe.wait_ge(lo_ready, i * (2 * UPC) + (u0 + 1))
                        products(u0 % RING, j, (h2T_hi, h2T_lo), (Q_FFN + c) % 2, j == 0, j == UPC - 1,
                                 UK * j).then_inc(unit_used, 1)
                        if c == 0 and j == 4:
                            act_transposes(i)
            act_transposes(NC_F)
            with pe.Fori(0, NC_D // 2) as i:
                for c in range(2):
                    q = Q_DOWN + c
                    if c == 0:
                        pe.wait_ge(emptied["act"], evac_count(Q_DOWN - 2))
                        pe.wait_ge(emptied["dve"], i + (evac_count(Q_DOWN) - 1))
                    else:
                        pe.wait_ge(act_full, NC_F)
                        pe.wait_ge(emptied["dve"], i * 2 + (evac_count(Q_DOWN) - 1))
                    for j in range(UPD):
                        u0 = U_DOWN + c * UPD + j
                        if c == 0 and j == UPD - 2:
                            pe.wait_ge(aT_lo, 2 * NC_F)
                        pe.wait_ge(lo_ready, i * (2 * UPD) + (u0 + 1))
                        products(u0 % RING, j, (actT_hi, actT_lo), q % 2, j == 0, j == UPD - 1,
                                 UK * j).then_inc(unit_used, 1)

        @block.scalar
        def _(act):
            def split(u):
                s = u % RING
                act.wait_ge(raw_ready[s], 16 * (u // RING + 1))
                if u >= RING:
                    act.wait_ge(unit_used, u - RING + 1)
                if u == U_GC:
                    act.activation(whi[:, s, 0, 0:KD * NGC], raw[:, s, 0, 0:KD * NGC], ACT.Copy).then_inc(hi_ready, 1)
                else:
                    act.activation(whi[:, s, :, :], raw[:, s, :, :], ACT.Copy).then_inc(hi_ready, 1)

            def split_in_loop(u0, rounds, units):
                s = u0 % RING
                act.wait_ge(raw_ready[s], rounds * 16 + 16 * (u0 // RING + 1))
                act.wait_ge(unit_used, units + (u0 - RING + 1))
                act.activation(whi[:, s, :, :], raw[:, s, :, :], ACT.Copy).then_inc(hi_ready, 1)

            def hi_of_transposed(n, b, dst, gain):
                act.wait_ge(t_full, n + 1)
                src = bank[b][:, :].rearrange("p (k s) -> p k s", k=UK)
                if gain is None:
                    act.activation(dst, src, ACT.Copy).then_inc(t_hi, 1)
                else:
                    for k in range(UK):
                        last = act.activation(dst[:, k, :], src[:, k, :], ACT.Copy, scale=gain[:, k:k + 1])
                    last.then_inc(t_hi, 1)

            def square(t, c, junk, done):
                if done:
                    act.wait_ge(squares, done)
                act.activation(junk[:, :], X[:, t, c * W:(c + 1) * W], ACT.Square,
                               accum_out=sumsq[:, t, c:c + 1]).then_inc(squares, 1)

            def root(n):
                act.wait_ge(mean_ready, n)
                act.activation(stat[:, 1, :], stat[:, 0, :], ACT.Sqrt).then_inc(root_ready, 1)

            def follow(v):
                q, j = CHUNK_OF.get(v, (0, 0))
                kind, i, _, n = CHUNKS[q]
                if j == n - 1 and kind in ("gate", "gc"):
                    act.wait_ge(unit_used, v + 1)
                    if kind == "gc":
                        act.wait_ge(rstd_ready, 1)
                        for t in range(TT):
                            last = act.activation(gsig[:, t, :], bank[2 * (q % 2) + t][:, 0:NGC], ACT.Sigmoid,
                                                  scale=rstd[:, t:t + 1])
                        last.then_inc(emptied["act"], 1)
                    else:
                        if i >= SIG:
                            act.wait_ge(emptied["dve"], evac_count(branch_q[i - SIG]))
                        for t in range(TT):
                            last = act.activation(sig[:, i % SIG, t, :], bank[2 * (q % 2) + t][:, :], ACT.Sigmoid,
                                                  scale=rstd[:, t:t + 1])
                        last.then_inc(emptied["act"], 1)
                mixer_step(v - U_MIX)
                for m in range(NC_D):
                    if v == merge_T_at(m):
                        for g in range(2):
                            hi_of_transposed(UPC + 2 * m + g, 4 + g, hT_hi[:, 4 * m + 2 * g:4 * m + 2 * g + 2, :], None)
                    if v == out_T_at(m):
                        for g in range(2):
                            k0 = 4 * m + 2 * g
                            hi_of_transposed(2 * UPC + 2 * m + g, 4 + g, h2T_hi[:, k0:k0 + 2, :],
                                             gainT[:, 1, k0:k0 + 2])
                        for t in range(TT):
                            square(t, m, bank[7], TT * NC_D + TT * m + t)

            def mixer_step(k):
                if k < 0:
                    return
                if MLP_SLOTS.get(k) == "up_k":
                    act.wait_ge(mlp_up, 1)
                    act.activation(hid_k[:, :, :, :], bank[6][:, 0:64].rearrange("p (a g n) -> p a g n", a=2, g=2),
                                   ACT.Gelu_apprx_tanh).then_inc(hid_ready, 1)
                if MLP_SLOTS.get(k) == "up_v":
                    act.wait_ge(mlp_up, 2)
                    src = bank[7][:, 0:64].rearrange("p (a g n) -> p a g n", a=2, g=2)
                    for r in range(4):
                        last = act.activation(hid_v[:, :, :, r, :], src, ACT.Gelu_apprx_tanh)
                    last.then_inc(hid_ready, 1)
                if k - 1 in SOFT_AT:
                    i = SOFT_AT[k - 1]
                    kind, pr = soft(i)
                    act.wait_ge(scores_sb, i + 1)
                    if kind == "cmp":
                        act.activation(sc[:, i % 2, 0, 0:S], sc[:, i % 2, 0, 0:S], ACT.Exp).then_inc(exps, 1)
                    else:
                        sm = small[:, i % 2, :, :, :]
                        if kind == "swa":
                            act.activation(sm[:, 3, :, :], sm[:, 2, :, :], ACT.Exp)
                        for h in range(2):
                            s = sc[:, i % 2, h, :]
                            act.activation(s[:, 0:P], s[:, 0:P], ACT.Exp, bias=sm[:, 0, 0, h:h + 1],
                                           accum_out=sm[:, 1, 0, h:h + 1])
                            last = act.activation(s[:, P:3 * P], s[:, P:3 * P], ACT.Exp, bias=sm[:, 0, 1, h:h + 1],
                                                  accum_out=sm[:, 1, 1, h:h + 1])
                        last.then_inc(exps, 1)
                if k in PROBS_T_AT:
                    i = PROBS_T_AT[k]
                    act.wait_ge(probsT_full, i + 1)
                    if soft(i)[0] == "cmp":
                        act.activation(pT[:, i % 2, 0, 0:S], bank[6][:, 0:S], ACT.Copy).then_inc(probsT, 1)
                    else:
                        act.activation(pT[:, i % 2, :, 0:P], bank[7][:, 0:S].rearrange("p (h s) -> p h s", h=2), ACT.Copy)
                        act.activation(pT[:, i % 2, :, P:3 * P], bank[6][:, :].rearrange("p (h s) -> p h s", h=2),
                                       ACT.Copy).then_inc(probsT, 1)
                for h, s in STICK.get(k - 1, []):
                    if s == 0:
                        act.wait_ge(z_ready, h + 1)
                        link(act, "act", act.activation(s_ln, s_z, ACT.Abs))
                        link(act, "act", act.activation(s_ln, s_ln, ACT.Exp, scale=-1.0))
                        act.activation(s_ln, s_ln, ACT.Ln, bias=1.0).then_inc(z_ln, 1)
                    if s == 4:
                        act.wait_ge(z_arg, h + 1)
                        if h >= 1:
                            act.wait_ge(z_w, h)
                        act.activation(s_surv, s_arg, ACT.Exp).then_inc(z_surv, 1)

            act.wait_ge(gains_full, 1)
            act.activation(gainT[:, :, :], bank[2][:, 0:4 * KD].rearrange("p (a k) -> p a k", a=4),
                           ACT.Copy).then_inc(gains_ready, 1)
            act.wait_ge(gains_ready, 1)
            for m in range(UPC):
                hi_of_transposed(m, 4 + m % 4, hT_hi[:, 2 * m:2 * m + 2, :], gainT[:, 0, 2 * m:2 * m + 2])
                split(m)
                act.wait_ge(x_ready[m // 2], 16)
                square(m % 2, m // 2, bank[3], m)
            root(1)
            with act.Fori(0, (N_QKV - 1) // 2) as i:
                for j in range(2 * UPC):
                    split_in_loop(UPC + j, i * (2 * UPC // RING), i * (2 * UPC))
            for u in range(U_GC, U_FFN):
                split(u)
                follow(u - LAG)

            def gate_silu(full, empty_up):
                act.wait_ge(unit_used, full)
                act.wait_ge(rstd_ready, 2)
                if empty_up is not None:
                    act.wait_ge(act_full, empty_up)
                for t in range(TT):
                    last = act.activation(silu[:, t, :], bank[2 * (Q_FFN % 2) + t][:, :], ACT.Silu,
                                          scale=rstd[:, t:t + 1])
                last.then_inc(emptied["act"], 1)

            for j in range(2 * UPC):
                split(U_FFN + j)
                if j < LAG or j == 2 + LAG:
                    follow(U_FFN + j - LAG)
                if j == 2 + LAG:
                    root(2)
                if j == UPC + LAG - 1:
                    gate_silu(U_FFN + UPC, None)
            with act.Fori(1, NC_F) as i:
                for j in range(2 * UPC):
                    split_in_loop(U_FFN + j, i * (2 * UPC // RING), i * (2 * UPC))
                    if j == UPC + LAG - 1:
                        gate_silu(i * (2 * UPC) + (U_FFN + UPC), i)
            def square_down(t, c):
                act.wait_ge(squares, c * TT + (2 * TT * NC_D + t))
                act.activation(bank[7][:, :], X[:, t, bass.ts(c, W)], ACT.Square,
                               accum_out=sumsq[:, t, bass.ds(c, 1)]).then_inc(squares, 1)

            with act.Fori(0, NC_D // 2) as i:
                for j in range(2 * UPD):
                    if j == UPD + LAG:
                        act.wait_ge(emptied["dve"], i * 2 + (evac_count(Q_DOWN)))
                    split_in_loop(U_DOWN + j, i * (2 * UPD // RING), i * (2 * UPD))
                    if j == UPD + LAG:
                        for t in range(TT):
                            square_down(t, i * 2)
                act.wait_ge(emptied["dve"], i * 2 + (evac_count(Q_DOWN) + 1))
                act.activation(stat[:, 5, :], ident[:, 0:TT], ACT.Copy)
                for t in range(TT):
                    square_down(t, i * 2 + 1)
            root(3)
            act.wait_ge(rstd_ready, 3)
            for n in range(NC_D):
                act.wait_ge(gained, n + 1)
                act.activation(X[:, 1, n * W:(n + 1) * W], X[:, 1, n * W:(n + 1) * W], ACT.Copy,
                               scale=rstd[:, 1:2]).then_inc(result[1], 1)

        @block.vector
        def _(dve):
            def chain(ins):
                link(dve, "dve", ins)

            def split_unit(slot, count, n=UK * W):
                dve.wait_ge(hi_ready, count)
                flat = [m[:, slot, :, :].rearrange("p k w -> p (k w)")[:, 0:n] for m in (wlo, raw, whi)]
                dve.tensor_tensor(flat[0], flat[1], flat[2].bitcast(F32), ALU.subtract).then_inc(lo_ready, 1)

            def split(u):
                split_unit(u % RING, u + 1, KD * NGC if u == U_GC else UK * W)

            def lo_of_transposed(n, b, lo, hi, gain):
                dve.wait_ge(t_hi, n + 1)
                src = bank[b][:, :].rearrange("p (k s) -> p k s", k=UK)
                if gain is None:
                    dve.tensor_tensor(lo, src, hi.bitcast(F32), ALU.subtract).then_inc(t_lo, 1)
                else:
                    for k in range(UK):
                        last = dve.scalar_tensor_tensor(lo[:, k, :], src[:, k, :], gain[:, k:k + 1],
                                                        hi[:, k, :].bitcast(F32), ALU.mult, ALU.subtract)
                    last.then_inc(t_lo, 1)

            def norm(n):
                dve.wait_ge(squares, 2 * NC_D * n)
                chain(dve.tensor_reduce(out=stat[:, 2, :], in_=sumsq[:, :, :], axis=AX_X, op=ALU.add))
                dve.tensor_scalar(stat[:, 0, :], stat[:, 2, :], 1.0 / D, EPS, ALU.mult, ALU.add).then_inc(mean_ready, 1)
                dve.wait_ge(root_ready, n)
                chain(dve.reciprocal(stat[:, 3, :], stat[:, 1, :]))
                chain(dve.tensor_tensor(stat[:, 4, :], stat[:, 3, :], stat[:, 3, :], ALU.mult))
                chain(dve.tensor_tensor(stat[:, 4, :], stat[:, 4, :], stat[:, 0, :], ALU.mult))
                chain(dve.tensor_scalar(stat[:, 4, :], stat[:, 4, :], -0.5, 1.5, ALU.mult, ALU.add))
                dve.tensor_tensor(rstd[:, :], stat[:, 3, :], stat[:, 4, :], ALU.mult).then_inc(rstd_ready, 1)

            def split_y(r, k, src):
                chain(dve.tensor_copy(yT_hi[:, r, k, :], src))
                return dve.tensor_tensor(yT_lo[:, r, k, :], src, yT_hi[:, r, k, :].bitcast(F32), ALU.subtract)

            def empty_projection(pair, cols):
                for t in range(TT):
                    last = dve.tensor_scalar(proj[:, t, cols], bank[2 * pair + t][:, :], rstd[:, t:t + 1], None, ALU.mult)
                last.then_inc(emptied["dve"], 1)

            def follow(v):
                q, j = CHUNK_OF.get(v, (0, 0))
                kind, i, _, n = CHUNKS[q]
                pair = q % 2
                if j == n - 1 and kind == "qkv":
                    dve.wait_ge(unit_used, v + 1)
                    empty_projection(pair, slice(i * W, (i + 1) * W))
                if j == n - 1 and kind == "branch":
                    s, c = i // NC_D, i % NC_D
                    dve.wait_ge(unit_used, v + 1)
                    dve.wait_ge(emptied["act"], evac_count(gate_q[i]))
                    cols = slice(c * W, (c + 1) * W)
                    for t in range(TT):
                        dst = merged[:, t, cols] if s == 0 else sig[:, i % SIG, t, :]
                        last = dve.tensor_tensor(dst, bank[2 * pair + t][:, :], sig[:, i % SIG, t, :], ALU.mult)
                    if s > 0:
                        chain(last)
                        last = dve.tensor_tensor(merged[:, :, cols], merged[:, :, cols], sig[:, i % SIG, :, :], ALU.add)
                    last.then_inc(emptied["dve"], 1)
                if j == n - 1 and kind == "out":
                    dve.wait_ge(unit_used, v + 1)
                    dve.wait_ge(x_again, 16)
                    for t in range(TT):
                        last = dve.tensor_tensor(X[:, t, i * W:(i + 1) * W], bank[2 * pair + t][:, :],
                                                 X[:, t, i * W:(i + 1) * W], ALU.add)
                    last.then_inc(emptied["dve"], 1)
                mixer_step(v - U_MIX)
                for m in range(NC_D):
                    for g in range(2):
                        k0 = 4 * m + 2 * g
                        if v == merge_T_at(m):
                            lo_of_transposed(UPC + 2 * m + g, 4 + g, hT_lo[:, k0:k0 + 2, :], hT_hi[:, k0:k0 + 2, :], None)
                        if v == out_T_at(m):
                            lo_of_transposed(2 * UPC + 2 * m + g, 4 + g, h2T_lo[:, k0:k0 + 2, :],
                                             h2T_hi[:, k0:k0 + 2, :], gainT[:, 1, k0:k0 + 2])

            def prepare(p):
                _, what, col, b = PREP[p]
                dve.wait_ge(prep_full, p + 1)
                src = bank[4 + b][:, :].rearrange("p (a s) -> p a s", a=2)
                if what == "q":
                    last = dve.tensor_scalar(qT[:, 2 * b:2 * b + 2, :], src, SCALE, None, ALU.mult)
                elif what == "sq":
                    last = dve.tensor_copy(sqT[:, 2 * b:2 * b + 2, :], src)
                elif what == "sk":
                    last = dve.tensor_copy(skT[:, 2 * b:2 * b + 2, :], src)
                elif what == "k":
                    dst = kz[1 if col == KWIN else 0]
                    for a in range(2):
                        last = dve.tensor_copy(dst[HD * a:HD * (a + 1), :, a, :], src[HD * a:HD * (a + 1), :, :])
                else:
                    m = 0 if col == KCMP else 1
                    for a in range(2):
                        half = slice(HD * a, HD * (a + 1))
                        for g in range(2):
                            tok = src[half, g, :].rearrange("p (n s) -> p s n", s=16)
                            for e in range(2):
                                ks = slice(8 * e, 8 * e + 8)
                                last = dve.tensor_tensor(
                                    blkT[m][half, ks, NP_CMP * g:NP_CMP * g + N_CMP],
                                    tok[:, a:16:2, e:e + N_CMP],
                                    gainT[half, 2 + m, ks].unsqueeze(2).to_broadcast([HD, 8, N_CMP]), ALU.add)
                last.then_inc(prep_done, 1)

            def masked_scores(i):
                kind, pr = soft(i)
                dve.wait_ge(scores_full, i + 1)
                if i >= 2:
                    dve.wait_ge(probsT_full, i - 1)
                if kind == "cmp":
                    s = sc[:, i % 2, 0, 0:S].rearrange("p (q h n) -> p q h n", q=TT, h=HEADS)
                    chain(dve.tensor_tensor(sc[:, i % 2, 0, 0:S], bank[4][:, 0:S],
                                            bias_c[:, :, :, :].rearrange("p q h n -> p (q h n)"), ALU.add))
                    chain(dve.tensor_reduce(out=csum[:, 0, :, :], in_=s, axis=AX_X, op=ALU.max))
                    dve.tensor_tensor(s, s, csum[:, 0, :, :].unsqueeze(3).to_broadcast([P, TT, HEADS, NP_CMP]),
                                      ALU.subtract).then_inc(scores_sb, 1)
                    return
                s, sm = sc[:, i % 2, :, :], small[:, i % 2, :, :, :]
                table = negdist_w if kind == "swa" else negdist
                for h in range(2):
                    dve.scalar_tensor_tensor(s[:, h, 0:P], table[:, P:S], slope(2 * pr + h),
                                             bank[5][:, h * P:(h + 1) * P], ALU.mult, ALU.add)
                    last = dve.scalar_tensor_tensor(s[:, h, P:3 * P], table[:, :], slope(2 * pr + h),
                                                    bank[4][:, h * S:(h + 1) * S], ALU.mult, ALU.add)
                chain(last)
                dve.tensor_reduce(out=sm[:, 0, 0, :], in_=s[:, :, 0:P], axis=AX_X, op=ALU.max, negate=True)
                last = dve.tensor_reduce(out=sm[:, 0, 1, :], in_=s[:, :, P:3 * P], axis=AX_X, op=ALU.max, negate=True)
                if kind == "swa":
                    chain(last)
                    sk = sinkb[:, 2 * pr:2 * pr + 2]
                    for t in range(TT):
                        last = dve.scalar_tensor_tensor(sm[:, 0, t, :], sk, -1.0, sm[:, 0, t, :], ALU.mult, ALU.min)
                    chain(last)
                    for t in range(TT):
                        last = dve.tensor_tensor(sm[:, 2, t, :], sk, sm[:, 0, t, :], ALU.add)
                last.then_inc(scores_sb, 1)

            def normalised(i):
                kind, pr = soft(i)
                dve.wait_ge(exps, i + 1)
                if kind == "cmp":
                    s = sc[:, i % 2, 0, 0:S].rearrange("p (q h n) -> p q h n", q=TT, h=HEADS)
                    valid = valid_c[:, :, :].unsqueeze(2).to_broadcast([P, TT, HEADS, NP_CMP])
                    chain(dve.tensor_tensor(s, s, valid, ALU.mult))
                    chain(dve.tensor_reduce(out=csum[:, 0, :, :], in_=s, axis=AX_X, op=ALU.add))
                    chain(dve.tensor_scalar(csum[:, 1, :, :], csum[:, 0, :, :], 1e-30, None, ALU.max))
                    chain(dve.reciprocal(csum[:, 2, :, :], csum[:, 1, :, :]))
                    gate = gsig[:, :, :].rearrange("p t (h b) -> p t h b", b=3)[:, :, :, 0]
                    chain(dve.tensor_tensor(csum[:, 0, :, :], csum[:, 2, :, :], gate, ALU.mult))
                    dve.tensor_tensor(s, s, csum[:, 0, :, :].unsqueeze(3).to_broadcast([P, TT, HEADS, NP_CMP]),
                                      ALU.mult).then_inc(probs, 1)
                    return
                s, sm = sc[:, i % 2, :, :], small[:, i % 2, :, :, :]
                if kind == "swa":
                    chain(dve.tensor_tensor(sm[:, 1, :, :], sm[:, 1, :, :], sm[:, 3, :, :], ALU.add))
                    chain(dve.reciprocal(sm[:, 5, :, :], sm[:, 1, :, :]))
                else:
                    chain(dve.reciprocal(sm[:, 4, :, :], sm[:, 1, :, :]))
                    b = 1 if kind == "sel" else 2
                    gate = gsig[:, :, :].rearrange("p t (h b) -> p t h b", b=3)[:, :, 2 * pr:2 * pr + 2, b]
                    chain(dve.tensor_tensor(sm[:, 5, :, :], sm[:, 4, :, :], gate, ALU.mult))
                for h in range(2):
                    dve.tensor_scalar(s[:, h, 0:P], s[:, h, 0:P], sm[:, 5, 0, h:h + 1], None, ALU.mult)
                    last = dve.tensor_scalar(s[:, h, P:3 * P], s[:, h, P:3 * P], sm[:, 5, 1, h:h + 1], None, ALU.mult)
                last.then_inc(probs, 1)

            def read_values(i):
                kind, pr = soft(i)
                dve.wait_ge(values_full, i + 1)
                src = bank[7][:, S:2 * S]
                if kind == "sel":
                    last = dve.tensor_copy(yacc[:, pr, :], src)
                elif kind == "win":
                    last = dve.tensor_tensor(yacc[:, pr, :], src, yacc[:, pr, :], ALU.add)
                elif kind == "swa":
                    last = split_y(1, pr, src)
                else:
                    for n in range(2):
                        acc = yacc[:, 2 * n:2 * n + 2, :]
                        chain(dve.tensor_tensor(acc, bank[7 - n][:, :].rearrange("p (a s) -> p a s", a=2), acc, ALU.add))
                        last = split_y(0, slice(2 * n, 2 * n + 2), acc)
                last.then_inc(values_read, 1)

            def mixer_step(k):
                if k < 0:
                    return
                if k in PREP_AT:
                    prepare(PREP_AT[k])
                if MLP_SLOTS.get(k) == "down_k":
                    dve.wait_ge(mlp_down, 1)
                    for a in range(2):
                        half = slice(HD * a, HD * (a + 1))
                        last = dve.tensor_copy(kcz[half, :, a, :], bank[6][half, 0:32].rearrange("p (g n) -> p g n", g=2))
                    last.then_inc(cmp_ready, 1)
                if MLP_SLOTS.get(k) == "down_v":
                    dve.wait_ge(mlp_down, 2)
                    dve.tensor_tensor(vz[:, :, :], bank[7][:, 0:HD].unsqueeze(1).to_broadcast([P, HEADS, HD]),
                                      head_mask[:, :].unsqueeze(2).to_broadcast([P, HEADS, HD]),
                                      ALU.mult).then_inc(cmp_ready, 1)
                if k in SOFT_AT:
                    masked_scores(SOFT_AT[k])
                if k - 2 in SOFT_AT:
                    normalised(SOFT_AT[k - 2])
                if k in VALUES_AT:
                    read_values(VALUES_AT[k])
                for h, s in STICK.get(k, []):
                    if s == 0:
                        dve.wait_ge(z_full, h + 1)
                        dve.tensor_scalar(s_z, bank[4 + h % 2][:, 0:3 * P], SB_SCALE, None, ALU.mult).then_inc(z_ready, 1)
                    if s == 4:
                        dve.wait_ge(z_cum, h + 1)
                        if h >= 1:
                            dve.wait_ge(z_surv, h)
                        dve.tensor_tensor(s_arg, s_z, bank[6][:, 0:3 * P], ALU.subtract).then_inc(z_arg, 1)
                    if s == 8:
                        dve.wait_ge(z_val, h + 1)
                        if h == 0:
                            dve.wait_ge(unit_used, BRANCH_END[NC_D - 1] + 1)
                        last = split_y(0, h, bank[7][:, 0:S])
                        last.then_inc(values_read, 1)
                for h, s in STICK.get(k - 2, []):
                    if s == 0:
                        dve.wait_ge(z_ln, h + 1)
                        if h >= 1:
                            dve.wait_ge(z_cum, h)
                        dve.scalar_tensor_tensor(s_sp, s_z, 0.0, s_ln, ALU.max, ALU.add).then_inc(z_sp, 1)
                        chain(dve.scalar_tensor_tensor(s_z, s_z, 0.0, s_ln, ALU.min, ALU.subtract))

            for m in range(UPC):
                ks = slice(2 * m, 2 * m + 2)
                lo_of_transposed(m, 4 + m % 4, hT_lo[:, ks, :], hT_hi[:, ks, :], gainT[:, 0, ks])
                split(m)
            norm(1)
            dve.wait_ge(rstd_ready, 1)
            with dve.Fori(0, (N_QKV - 1) // 2) as i:
                for c in range(2):
                    for j in range(UPC):
                        u0 = UPC + c * UPC + j
                        split_unit(u0 % RING, i * (2 * UPC) + (u0 + 1))
                        if j == LAG - 1:
                            dve.wait_ge(unit_used, i * (2 * UPC) + UPC * (1 + c))
                            empty_projection(c, bass.ts(i * 2 + c, W))
            dve.wait_ge(consts_ready, 1)
            dve.wait_ge(sinks_ready, 16)
            for u in range(U_GC, U_FFN):
                split(u)
                if u == U_MIX + LAG:
                    dve.wait_ge(zeros_ready, 1)
                    dve.wait_ge(emptied["act"], 1)
                follow(u - LAG)

            def gated(full, silus):
                dve.wait_ge(unit_used, full)
                dve.wait_ge(emptied["act"], silus)
                for t in range(TT):
                    last = dve.scalar_tensor_tensor(act_rows[:, t, :], bank[2 * ((Q_FFN + 1) % 2) + t][:, :],
                                                    rstd[:, t:t + 1], silu[:, t, :], ALU.mult, ALU.mult)
                last.then_inc(act_full, 1)

            def act_columns(g, done, rows_of):
                src = bank[4 + g][:, :].rearrange("p (k s) -> p k s", k=UK)
                dve.wait_ge(aT_full, done + 1)
                dve.tensor_scalar(actT_hi[:, rows_of, :], src, 1.0, None, ALU.mult).then_inc(aT_hi, 1)
                dve.wait_ge(aT_hi, done + 1)
                dve.tensor_tensor(actT_lo[:, rows_of, :], src, actT_hi[:, rows_of, :].bitcast(F32),
                                  ALU.subtract).then_inc(aT_lo, 1)

            for j in range(2 * UPC):
                split(U_FFN + j)
                if j < LAG or j == 2 + LAG:
                    follow(U_FFN + j - LAG)
                if j == 2 + LAG:
                    norm(2)
                    dve.wait_ge(rstd_ready, 2)
            silus = evac_count(Q_FFN)
            with dve.Fori(1, NC_F) as i:
                for j in range(2 * UPC):
                    split_unit((U_FFN + j) % RING, i * (2 * UPC) + (U_FFN + j + 1))
                    if j == LAG - 1:
                        gated(i * (2 * UPC) + U_FFN, i + (silus - 1))
                    if j in (UPC - 1, UPC):
                        g = j - UPC + 1
                        act_columns(g, i * 2 + (g - 2), bass.ds(i * 4 + (2 * g - 4), 2))
            gated(U_DOWN, silus + NC_F - 1)
            for g in range(2):
                act_columns(g, 2 * (NC_F - 1) + g, slice(KF - 4 + 2 * g, KF - 2 + 2 * g))

            def add_down(c, cols, full):
                dve.wait_ge(unit_used, full)
                for t in range(TT):
                    last = dve.tensor_tensor(X[:, t, cols], bank[2 * ((Q_DOWN + c) % 2) + t][:, :], X[:, t, cols], ALU.add)
                last.then_inc(emptied["dve"], 1)

            with dve.Fori(0, NC_D // 2) as i:
                for j in range(2 * UPD):
                    split_unit((U_DOWN + j) % RING, i * (2 * UPD) + (U_DOWN + j + 1))
                    if j == UPD + LAG - 1:
                        add_down(0, bass.ts(i * 2, W), i * (2 * UPD) + (U_DOWN + UPD))
                add_down(1, bass.ts(i * 2 + 1, W), i * (2 * UPD) + (U_DOWN + 2 * UPD))
            norm(3)
            dve.wait_ge(rstd_ready, 3)
            for n in range(NC_D):
                dve.wait_ge(gained, n + 1)
                dve.tensor_scalar(X[:, 0, n * W:(n + 1) * W], X[:, 0, n * W:(n + 1) * W], rstd[:, 0:1], None,
                                  ALU.mult).then_inc(result[0], 1)


_OUT = (1, S, D)


def kernel(x, norm_mix, w_in, swa_sinks, cmp_pe_k, cmp_w1_k, cmp_w2_k, cmp_pe_v, cmp_w1_v, cmp_w2_v,
           w_branch_swa, w_branch_sb, w_branch_nsa, w_out, norm_ffn, w_gate, w_up, w_down, norm_final):
    import numpy as np
    import concourse.bacc as bacc
    from concourse.bass_utils import run_bass_kernel_spmd

    arrays = {
        "x": x, "norm_mix": norm_mix, "w_in": w_in, "sinks": swa_sinks,
        "pe_k": cmp_pe_k, "w1_k": cmp_w1_k, "w2_k": cmp_w2_k, "pe_v": cmp_pe_v, "w1_v": cmp_w1_v, "w2_v": cmp_w2_v,
        "w_br_a": w_branch_swa, "w_br_b": w_branch_sb, "w_br_c": w_branch_nsa, "w_out": w_out,
        "norm_ffn": norm_ffn, "w_gate": w_gate, "w_up": w_up, "w_down": w_down, "norm_final": norm_final,
    }
    arrays = {"in_" + k: np.ascontiguousarray(v) for k, v in arrays.items()}
    nc = bacc.Bacc("TRN2", target_bir_lowering=False, num_devices=1)
    args = []
    for name, a in arrays.items():
        ap = nc.dram_tensor(name, a.shape, mybir.dt.from_np(a.dtype), kind="ExternalInput").ap()
        args.append(ap if name == "in_norm_final" else ap[0])
    res = nc.dram_tensor("out", _OUT, F32, kind="ExternalOutput").ap()
    build_layer(nc, *args, res[0])
    r = run_bass_kernel_spmd(nc, [arrays], core_ids=[0])
    return r.results[0]["out"]
```

```python
from contextlib import ExitStack

import concourse.bass as bass
from concourse import mybir

F32 = mybir.dt.float32
F32R = mybir.dt.float32r
ALU = mybir.AluOpType
ACT = mybir.ActivationFunctionType
AX_X = mybir.AxisListType.X

P = 128
TT = 2
S = TT * P
D = 2048
KD = D // P
W = 512
NC_D = D // W
FF = 5632
KF = FF // P
NC_F = FF // W
HD = 64
HEADS = 8
PAIRS = HEADS // 2
SB_HEADS = 4
N_CMP = 15
NP_CMP = 16
MLP_W = 256
EPS = 1e-6
NEG = -1.0e35
SCALE = 0.125
SB_SCALE = float(128) ** -0.5

QA, KA, VA = 0, 512, 640
QB, KB, VB = 768, 1280, 1792
QC, KCMP, VCMP, KSEL, VSEL, KWIN, VWIN = 2304, 2816, 2944, 3072, 3200, 3328, 3456
GC, NGC = 3584, 24
GATES = 3608
N_PROJ = GATES
WQ = 452

UK = 2
RING = 4
UPC = KD // UK
N_QKV = -(-N_PROJ // WQ)
UM = KD // 4
U_MIX = N_QKV * UPC
U_OUT = U_MIX + 12 * UPC + 12 * 2 + 2 * UM
U_FFN = U_OUT + NC_D * UPC
U_DOWN = U_FFN + 2 * NC_F * UPC
UPD = KF // UK
U_END = U_DOWN + NC_D * UPD
LAG = 3
SIG = 6

X_PIECES = [(0, W // 2), (W // 2, W)] + [(_c * W, (_c + 1) * W) for _c in range(1, NC_D)]

GATE_COL = [GATES + 2 * D, GATES, GATES + D]


def mix_plan():
    plan, u = [], U_MIX
    for g in range(12):
        plan.append(("gate", g, u))
        u += UPC
        if g == 0:
            for n in range(2):
                plan.append(("mlp", n, u))
                u += UM
        if g >= 5:
            plan.append(("branch", g - 5, u))
            u += 2
    for b in range(7, 12):
        plan.append(("branch", b, u))
        u += 2
    assert u == U_OUT
    return plan


MIX = mix_plan()
CHUNKS = [("qkv", c, c * UPC, UPC) for c in range(N_QKV)]
CHUNKS += [(k, i, u, {"gate": UPC, "mlp": UM, "branch": 2}[k]) for k, i, u in MIX]
CHUNKS += [("out", c, U_OUT + c * UPC, UPC) for c in range(NC_D)]
Q_FFN = len(CHUNKS)
Q_DOWN = Q_FFN + 2 * NC_F
CHUNK_OF = {}
for _q, (_k, _i, _u, _n) in enumerate(CHUNKS):
    for _j in range(_n):
        CHUNK_OF[_u + _j] = (_q, _j)
MLP_END = {i: u + UM - 1 for k, i, u in MIX if k == "mlp"}
BRANCH_END = {i: u + 1 for k, i, u in MIX if k == "branch"}

CMP = 8
N_SOFT = 13


def soft(i):
    if i < CMP:
        return ("sel", "win")[i % 2], i // 2
    return ("cmp", None) if i == CMP else ("swa", i - CMP - 1)


def soft_slot(i):
    return 17 + 3 * i if i <= CMP else 20 + 3 * i


SOFT_AT = {soft_slot(i): i for i in range(N_SOFT)}
PROBS_T_AT = {soft_slot(i) + 5: i for i in range(N_SOFT)}
VALUES_AT = {soft_slot(i) + 7: i for i in range(N_SOFT)}
PREP = [(0, "c", KCMP, 0), (1, "c", VCMP, 1), (2, "q", QC, 0), (3, "q", QC, 1), (4, "k", KSEL, 0), (5, "k", KWIN, 1),
        (42, "q", QA, 0), (43, "q", QA, 1), (44, "k", KA, 0),
        (58, "sq", QB, 0), (59, "sq", QB, 1), (60, "sk", KB, 0), (61, "sk", KB, 1)]
PREP_AT = {p[0]: n for n, p in enumerate(PREP)}
NSA_GATES_SLOT = 3
DVE_OUT = [(NC_D - 1, 0), (0, NC_D - 1)]
ACT_OUT = [(1, 2), (1, 2)]


def stick_slot(h, step):
    return 84 + 6 * h + step


STICK = {}
for _h in range(SB_HEADS):
    for _s in (0, 5, 9):
        STICK.setdefault(stick_slot(_h, _s), []).append((_h, _s))


def merge_T_at(m):
    return BRANCH_END[2 * NC_D + m] + LAG


def out_T_at(m):
    return U_OUT + (m + 1) * UPC - 1 + LAG


def evac_engine(q):
    if q < Q_FFN:
        return "act" if CHUNKS[q][0] in ("gate", "mlp") else "dve"
    return ("act", "up")[(q - Q_FFN) % 2] if q < Q_DOWN else "dve"


def evac_count(q):
    return sum(evac_engine(r) == evac_engine(q) for r in range(q + 1))


def width(u):
    return min(WQ, N_PROJ - u // UPC * WQ) if u < U_MIX else W


def landed(u):
    units = range(u % RING, u + 1, RING)
    twice = [v for v in units if v in CHUNK_OF and CHUNKS[CHUNK_OF[v][0]][0] == "branch"
             and CHUNKS[CHUNK_OF[v][0]][1] < 2 * NC_D]
    return 16 * (len(units) + len(twice))


def slope(h):
    return 2.0 ** -(h + 1)


def head(pr, a):
    return pr + PAIRS * a


def build_layer(nc, x_in, norm_mix, w_in, sinks, pe_k, w1_k, w2_k, pe_v, w1_v, w2_v,
                w_br_a, w_br_b, w_br_c, w_out, norm_ffn, w_gate, w_up, w_down, norm_final, out):
    ctx = ExitStack()
    with ctx:
        top = [(nc.sbuf_base + 31) // 32 * 32]

        def at(name, shape, offset, dt=F32):
            return nc.alloc_sbuf_tensor_at(name, [P] + shape, dt, offset=offset)

        def place(name, shape, dt=F32):
            n = 4
            for s in shape:
                n *= s
            n = (n + 31) // 32 * 32
            t = at(name, shape, top[0], dt)
            top[0] += n
            assert top[0] <= nc.sbuf_top, name
            return t

        raw = place("raw_ring", [RING, UK, W])
        whi = place("weight_hi_ring", [RING, UK, W], F32R)
        wlo = place("weight_lo_ring", [RING, UK, W], F32R)
        ident = place("identity", [P])
        gainT = place("gains_T", [4, KD])
        sumsq = place("sumsq", [TT, NC_D])
        stat = place("stat", [6, TT])
        rstd = place("rstd", [TT])
        X = place("x", [TT, D])

        low = top[0]
        hT_hi = place("hT_hi", [KD, S], F32R)
        hT_lo = place("hT_lo", [KD, S], F32R)
        proj = place("proj", [TT, N_PROJ])
        sig = place("sigmoid_gates", [SIG, TT, W])
        sc = place("scores", [2, 2, 3 * P])
        pT = place("probs_T", [2, 2, 3 * P])
        mid = top[0]
        merged = place("merged", [TT, D])
        yT_hi = place("yT_hi", [2, 4, S], F32R)
        yT_lo = place("yT_lo", [2, 4, S], F32R)
        negdist = place("negdist", [S])
        negdist_w = place("negdist_window", [S])
        bias_c = place("bias_compressed", [TT, HEADS, NP_CMP])
        nd_c = place("negdist_compressed", [TT, NP_CMP])
        valid_c = place("valid_compressed", [TT, NP_CMP])
        kcz = place("kc_zero_padded", [2, NP_CMP])
        hid = place("hidden", [MLP_W])
        hid_k = place("hidden_k", [2, 2, NP_CMP])
        hid_v = place("hidden_v", [2, PAIRS, 2, NP_CMP])
        w2k = place("w2_k_twice", [2, 2, HD])
        w2v = place("w2_v", [2, HD])
        vz = place("vc_block_diagonal", [HEADS, HD])
        head_mask = place("head_mask", [HEADS])
        gsig = place("nsa_gates", [TT, NGC])
        sinkb = place("sinks", [HEADS])
        small = place("softmax_small", [2, 6, 2, 2])
        csum = place("cmp_small", [3, TT, HEADS])
        strict = place("strict_mask", [3 * P])
        later = place("later", [P])
        ones = place("ones", [P])

        h2T_hi = at("h2T_hi", [KD, S], mid, F32R)
        h2T_lo = at("h2T_lo", [KD, S], mid + 4 * KD * S, F32R)
        actT_hi = at("actT_hi", [KF, S], low, F32R)
        actT_lo = at("actT_lo", [KF, S], low + 4 * KF * S, F32R)
        silu = at("silu", [TT, W], low + 8 * KF * S)
        act_rows = at("act_rows", [TT, W], low + 8 * KF * S + 4 * TT * W)
        assert low + 8 * KF * S + 8 * TT * W <= mid
        gfin = at("norm_final", [D], mid)

        xs = X[:, :, :].rearrange("p t d -> p (t d)")
        qT = xs[:, 0:1024].rearrange("p (r s) -> p r s", r=PAIRS)
        q_rows = xs[:, 2048:3072].rearrange("p (t r a d) -> p t r a d", t=TT, r=PAIRS, a=2)
        kz = [xs[:, 1024 + 512 * n:1536 + 512 * n].rearrange("p (a s) -> p a s", a=2) for n in range(2)]
        blkT = xs[:, 3072:4096].rearrange("p (k m c) -> p k m c", k=KD, m=2)
        sqT = xs[:, 2048:3072].rearrange("p (h s) -> p h s", h=SB_HEADS)
        skT = xs[:, 3072:4096].rearrange("p (h s) -> p h s", h=SB_HEADS)
        rows = sig[:, 0, 0, :].rearrange("p (a c) -> p a c", a=4)
        yacc = merged[:, 0, 0:PAIRS * S].rearrange("p (r s) -> p r s", r=PAIRS)
        blk_hi, blk_lo = (m[:, :, :, :].rearrange("p r k s -> p (r k s)").rearrange("p (k c) -> p k c", k=KD)
                          for m in (yT_hi, yT_lo))
        s_z = sc[:, 0, 1, :]
        s_ln = sc[:, 1, 0, :]
        s_sp = sc[:, 1, 1, :]
        s_arg = pT[:, 0, 0, :]
        s_surv = pT[:, 0, 1, :]
        s_w = pT[:, 1, 0, :]

        bank = [ctx.enter_context(nc.psum_tensor(f"bank{i}", [P, W], F32)) for i in range(8)]

        def sem(name):
            return ctx.enter_context(nc.semaphore(name))

        raw_ready = [sem(f"raw_ready{i}") for i in range(RING)]
        hi_ready = sem("hi_ready")
        lo_ready = sem("lo_ready")
        unit_used = sem("unit_used")
        emptied = {"act": sem("emptied_by_act"), "dve": sem("emptied_by_dve")}
        x_ready = [sem(f"x_ready{i}") for i in range(len(X_PIECES))]
        norm_row_ready = sem("norm_row_ready")
        rows_ready = sem("rows_ready")
        ident_ready = sem("ident_ready")
        gains_full = sem("gains_full")
        gains_ready = sem("gains_ready")
        t_full = sem("transposes_full")
        t_hi = sem("transposed_hi")
        t_lo = sem("transposed_lo")
        squares = sem("squares")
        mean_ready = sem("mean_ready")
        root_ready = sem("root_ready")
        rstd_ready = sem("rstd_ready")
        x_again = sem("x_again")
        consts_ready = sem("consts_ready")
        zeros_ready = sem("zeros_ready")
        w2_ready = sem("w2_ready")
        sinks_ready = sem("sinks_ready")
        prep_full = sem("prep_full")
        prep_done = sem("prep_done")
        q_rows_ready = sem("q_rows_ready")
        nsa_gates = sem("nsa_gates_ready")
        blk_ready = sem("blk_ready")
        hidT_full = sem("hiddenT_full")
        hidT_ready = sem("hiddenT_ready")
        mlp_down = sem("mlp_down")
        cmp_ready = sem("compressed_ready")
        scores_full = sem("scores_full")
        scores_sb = sem("scores_masked")
        exps = sem("exps")
        probs = sem("probs")
        probsT_full = sem("probsT_full")
        probsT = sem("probsT")
        values_full = sem("values_full")
        values_read = sem("values_read")
        z_full = sem("stick_z_full")
        z_ready = sem("stick_z_ready")
        z_ln = sem("stick_ln")
        z_sp = sem("stick_softplus")
        z_spm = sem("stick_softplus_masked")
        z_cum = sem("stick_cum_full")
        z_arg = sem("stick_arg")
        z_surv = sem("stick_surv")
        z_w = sem("stick_weights")
        z_val = sem("stick_values_full")
        act_full = sem("act_rows_ready")
        aT_full = sem("actT_full")
        aT_hi = sem("actT_hi_ready")
        added = sem("result_added")
        tile0_full = sem("token_tile0_full")
        aT_lo = sem("actT_ready")
        gfin_ready = sem("gfin_ready")
        gained = sem("gained")
        scaled = {"dve": sem("scaled_by_dve"), "act": sem("scaled_by_act")}
        stored = sem("stored")
        dve_step = sem("dve_step")
        act_step = sem("act_step")
        pool_step = sem("pool_step")
        steps = {"dve": 0, "act": 0, "pool": 0}
        step_sem = {"dve": dve_step, "act": act_step, "pool": pool_step}

        def link(eng, name, ins):
            steps[name] += 1
            ins.then_inc(step_sem[name], 1)
            eng.wait_ge(step_sem[name], steps[name])

        def blocks(w):
            return w.rearrange("(k p) n -> p k n", p=P)

        win_b, wout_b, wg_b, wu_b, wd_b = (blocks(w) for w in (w_in, w_out, w_gate, w_up, w_down))
        br_w = [w_br_c, w_br_a]
        x_b = x_in.rearrange("(t p) d -> p t d", p=P)
        out_b = out.rearrange("(t p) d -> p t d", p=P)

        branch_q = {CHUNKS[q][1]: q for q in range(Q_FFN) if CHUNKS[q][0] == "branch"}
        gate_q = {CHUNKS[q][1]: q for q in range(Q_FFN) if CHUNKS[q][0] == "gate"}
        mlp_q = {CHUNKS[q][1]: q for q in range(Q_FFN) if CHUNKS[q][0] == "mlp"}
        out_q = {CHUNKS[q][1]: q for q in range(Q_FFN) if CHUNKS[q][0] == "out"}

        block = ctx.enter_context(nc.Block())

        @block.sync
        def _(sp):
            def load(slot, src):
                sp.dma_start(raw[:, slot, :, :], src).then_inc(raw_ready[slot], 16)

            def free(count):
                sp.wait_ge(lo_ready, count)

            def straight(u):
                q, j = CHUNK_OF[u]
                kind, i, _, _ = CHUNKS[q]
                if u >= RING:
                    free(u - RING + 1)
                if kind == "mlp":
                    w1 = blocks((w1_k, w1_v)[i])[:, 4 * j:4 * j + 4, :]
                    sp.dma_start(raw[:, u % RING, :, :].rearrange("p k (a w) -> p (k a) w", a=2), w1)\
                      .then_inc(raw_ready[u % RING], 16)
                    return
                if kind == "qkv":
                    w = min(WQ, N_PROJ - i * WQ)
                    sp.dma_start(raw[:, u % RING, :, 0:w], win_b[:, UK * j:UK * j + UK, i * WQ:i * WQ + w])\
                      .then_inc(raw_ready[u % RING], 16)
                    return
                ks = slice(UK * j, UK * j + UK)
                if kind == "gate":
                    c = GATE_COL[i // NC_D] + (i % NC_D) * W
                    src = win_b[:, ks, c:c + W]
                elif kind == "branch":
                    c = (i % NC_D) * W
                    if i // NC_D < 2:
                        branch_in_pair_order(u, i // NC_D, j, c)
                        return
                    src = blocks(w_br_b)[:, ks, c:c + W]
                else:
                    src = wout_b[:, ks, i * W:(i + 1) * W]
                load(u % RING, src)

            def branch_in_pair_order(u, s, j, c):
                src = br_w[s][:, c:c + W].rearrange("(a k p) n -> a p k n", a=2, p=HD)[:, :, UK * j:UK * j + UK, :]
                for a in range(2):
                    sp.dma_start(raw[HD * a:HD * (a + 1), u % RING, :, :], src[a]).then_inc(raw_ready[u % RING], 16)

            def xload(n):
                cols = slice(X_PIECES[n][0], X_PIECES[n][1])
                sp.dma_start(X[:, :, cols], x_b[:, :, cols]).then_inc(x_ready[n], 16)

            for n in range(RING):
                xload(n)
                straight(n)
            xload(RING)
            for u in range(RING, UPC):
                straight(u)
            with sp.Fori(0, (N_QKV - 2) // 2) as i:
                for c in range(2):
                    for j in range(UPC):
                        u0 = UPC + c * UPC + j
                        sp.wait_ge(lo_ready, i * (2 * UPC) + (u0 - RING + 1))
                        sp.dma_start(raw[:, u0 % RING, :, 0:WQ],
                                     win_b[:, UK * j:UK * j + UK, bass.ds(i * (2 * WQ) + (1 + c) * WQ, WQ)])\
                          .then_inc(raw_ready[u0 % RING], 16)
            for u in range(U_MIX - UPC, U_FFN):
                straight(u)
            with sp.Fori(0, NC_F) as i:
                for c, w in enumerate((wg_b, wu_b)):
                    for j in range(UPC):
                        u0 = U_FFN + c * UPC + j
                        sp.wait_ge(lo_ready, i * (2 * UPC) + (u0 - RING + 1))
                        load(u0 % RING, w[:, UK * j:UK * j + UK, bass.ts(i, W)])
            with sp.Fori(0, NC_D // 2) as i:
                for c in range(2):
                    for j in range(UPD):
                        u0 = U_DOWN + c * UPD + j
                        sp.wait_ge(lo_ready, i * (2 * UPD) + (u0 - RING + 1))
                        load(u0 % RING, wd_b[:, UK * j:UK * j + UK, bass.ts(i * 2 + c, W)])
            for t in range(TT):
                for n in range(NC_D // 2):
                    for name, c in (("dve", DVE_OUT[t][n]), ("act", ACT_OUT[t][n])):
                        sp.wait_ge(scaled[name], t * NC_D // 2 + n + 1)
                        sp.dma_start(out_b[:, t, c * W:(c + 1) * W], X[:, t, c * W:(c + 1) * W]).then_inc(stored, 16)
            sp.wait_ge(stored, 16 * TT * NC_D)

        @block.gpsimd
        def _(pool):
            def select(t, pattern, base, cm, op, fill):
                return pool.affine_select(out=t, in_=t, compare_op=op, fill=fill, base=base,
                                          pattern=pattern, channel_multiplier=cm)

            link(pool, "pool", pool.memset(ident[:, :], 0.0))
            select(ident[:, :], [[-1, P]], 0, 1, ALU.not_equal, 1.0).then_inc(ident_ready, 1)
            pool.iota(negdist[:, :], pattern=[[1, S]], base=-P, channel_multiplier=-1,
                      allow_small_or_imprecise_dtypes=True)
            link(pool, "pool", pool.iota(nd_c[:, :, :], pattern=[[-P, TT], [NP_CMP, NP_CMP]], base=31,
                                         channel_multiplier=-1, allow_small_or_imprecise_dtypes=True))
            select(nd_c[:, :, :], [[P, TT], [-NP_CMP, NP_CMP]], -31, 1, ALU.is_ge, NEG)
            link(pool, "pool", select(negdist[:, :], [[-1, S]], P, 1, ALU.is_ge, NEG))
            pool.affine_select(out=negdist_w[:, :], in_=negdist[:, :], compare_op=ALU.is_ge, fill=NEG, base=-1,
                               pattern=[[1, S]], channel_multiplier=-1)
            for h in range(HEADS):
                pool.tensor_scalar(bias_c[:, :, h, :], nd_c[:, :, :], slope(head(h // 2, h % 2)), None, ALU.mult)
            pool.memset(valid_c[:, :, :], 1.0)
            pool.memset(strict[:, :], 1.0)
            pool.memset(later[:, :], 1.0)
            pool.memset(ones[:, :], 1.0)
            pool.memset(kcz[:, :, :], 0.0)
            pool.memset(yT_hi[:, :, :, :].bitcast(F32), 0.0)
            pool.memset(yT_lo[:, :, :, :].bitcast(F32), 0.0)
            link(pool, "pool", pool.memset(head_mask[:, :], 1.0))
            select(valid_c[:, :, :], [[P, TT], [-NP_CMP, NP_CMP]], -31, 1, ALU.is_ge, 0.0)
            select(strict[:, 0:P], [[1, P]], 0, -1, ALU.is_gt, 0.0)
            select(strict[:, 2 * P:3 * P], [[1, P]], 0, -1, ALU.is_gt, 0.0)
            select(later[:, :], [[-1, P]], 0, 1, ALU.is_gt, 0.0)
            link(pool, "pool", select(head_mask[:, :], [[-NP_CMP, HEADS]], 0, 1, ALU.is_ge, 0.0))
            select(head_mask[:, :], [[NP_CMP, HEADS]], NP_CMP - 1, -1, ALU.is_ge, 0.0).then_inc(consts_ready, 1)

            for a, src in enumerate((norm_ffn.rearrange("(k p) -> k p", p=P), pe_k.rearrange("(k a) d -> k (a d)", a=2),
                                     pe_v.rearrange("(k a) d -> k (a d)", a=2))):
                pool.dma_start(rows[0:KD, 1 + a, :], src).then_inc(rows_ready, 16)
            w2k_src = w2_k.rearrange("(k p) d -> p k d", p=P)
            pool.dma_start(w2k[:, :, 0, :], w2k_src).then_inc(w2_ready, 16)
            pool.dma_start(w2k[:, :, 1, :], w2k_src).then_inc(w2_ready, 16)
            pool.dma_start(w2v[:, :, :], w2_v.rearrange("(k p) d -> p k d", p=P)).then_inc(w2_ready, 16)
            pool.dma_start(sinkb[:, :], sinks.partition_broadcast(P)).then_inc(sinks_ready, 16)

            pool.wait_ge(t_lo, UPC)
            pool.wait_ge(squares, 2 * NC_D)
            pool.memset(xs[:, 1024:2048], 0.0)
            pool.memset(xs[:, 3072:4096], 0.0).then_inc(zeros_ready, 1)

            for n, col in enumerate((QC, QA)):
                pool.wait_ge(emptied["dve"], N_QKV) if n == 0 else pool.wait_ge(prep_done, 4)
                for t in range(TT):
                    heads = proj[:, t, col:col + HEADS * HD].rearrange("p (a r d) -> p r a d", a=2, r=PAIRS)
                    last = pool.tensor_copy(q_rows[:, t, :, :, :], heads)
                last.then_inc(q_rows_ready, 1)

            for h in range(SB_HEADS):
                pool.wait_ge(z_sp, h + 1)
                pool.tensor_tensor(s_sp, s_sp, strict[:, :], ALU.mult).then_inc(z_spm, 1)
                pool.wait_ge(z_surv, h + 1)
                if h >= 1:
                    pool.wait_ge(z_val, h)
                pool.tensor_tensor(s_w, s_surv, strict[:, :], ALU.mult).then_inc(z_w, 1)
                if h == SB_HEADS - 1:
                    pool.dma_start(X[:, :, :], x_b).then_inc(x_again, 16)

            pool.wait_ge(unit_used, U_DOWN)
            pool.dma_start(gfin[:, :], norm_final.partition_broadcast(P)).then_inc(gfin_ready, 16)
            pool.wait_ge(gfin_ready, 16)
            for n in range(NC_D - 1):
                pool.wait_ge(squares, 2 * TT * NC_D + TT * (n + 1))
                for t in range(TT):
                    last = pool.tensor_tensor(X[:, t, n * W:(n + 1) * W], X[:, t, n * W:(n + 1) * W],
                                              gfin[:, n * W:(n + 1) * W], ALU.mult)
                last.then_inc(gained, 1)

        @block.tensor
        def _(pe):
            def transpose(dst, src, n=P):
                return pe.transpose(dst, src, ident[0:n, 0:n])

            def products(slot, lhs, pair, first, last, k0, width=W, half=False,
                         tiles=tuple(range(TT))):
                l_hi, l_lo = lhs
                order = [(k, t) for t in range(TT) for k in range(UK)] if half else \
                    [(k, t) for k in range(UK) for t in tiles]
                for k, t in order:
                    dst = bank[2 * pair + t][:, 0:width]
                    x_hi, x_lo = (m[:, k0 + k, t * P:(t + 1) * P] for m in (l_hi, l_lo))
                    w_hi, w_lo = (m[:, slot, k, 0:width] for m in (whi, wlo))
                    pe.matmul(dst, x_hi, w_hi, start=first and k == 0, stop=False)
                    pe.matmul(dst, x_hi, w_lo, start=False, stop=False)
                    m = pe.matmul(dst, x_lo, w_hi, start=False, stop=last and k == UK - 1)
                    if half and (k, t) == (UK - 1, 0):
                        m.then_inc(tile0_full, 1)
                return m

            def unit(u, lhs, q, j, n, width=W):
                pe.wait_ge(lo_ready, u + 1)
                m = products(u % RING, lhs, q % 2, j == 0, j == n - 1, UK * j, width,
                             half=q == Q_FFN + 1 and j == n - 1)
                m.then_inc(unit_used, 1)

            def pair_free(q):
                if q >= 2:
                    how = evac_engine(q - 2)
                    pe.wait_ge(emptied[how], evac_count(q - 2))

            def straight(u):
                q, j = CHUNK_OF[u]
                kind, i, _, n = CHUNKS[q]
                if j == 0:
                    pair_free(q)
                    if q == 1:
                        pe.wait_ge(squares, 2 * NC_D)
                if kind == "mlp":
                    if j == 0:
                        pe.wait_ge(blk_ready, 1)
                    pe.wait_ge(lo_ready, u + 1)
                    h_, l_ = (w[:, u % RING, :, :].rearrange("p k (a w) -> p (k a) w", a=2) for w in (whi, wlo))
                    dst = bank[2 * (q % 2)][:, 0:MLP_W]
                    for k in range(4):
                        x_hi, x_lo = (m[:, 4 * j + k, :] for m in (blk_hi, blk_lo))
                        pe.matmul(dst, x_hi, h_[:, k, :], start=j == 0 and k == 0, stop=False)
                        pe.matmul(dst, x_hi, l_[:, k, :], start=False, stop=False)
                        m = pe.matmul(dst, x_lo, h_[:, k, :], start=False, stop=j == n - 1 and k == 3)
                    m.then_inc(unit_used, 1)
                    return
                if kind == "branch":
                    s = i // NC_D
                    pe.wait_ge(values_read, (CMP + 1, N_SOFT, N_SOFT + SB_HEADS)[s])
                    lhs = (yT_hi[:, s % 2, :, :], yT_lo[:, s % 2, :, :])
                elif kind == "out":
                    lhs = (hT_hi, hT_lo)
                    if i == 0:
                        pe.wait_ge(t_lo, UPC + j + 1)
                else:
                    lhs = (hT_hi, hT_lo)
                    if q == 0:
                        pe.wait_ge(t_lo, j + 1)
                unit(u, lhs, q, j, n, min(WQ, N_PROJ - i * WQ) if kind == "qkv" else W)

            def transposes_of_rows(n, b, src):
                for k in range(UK):
                    for t in range(TT):
                        m = transpose(bank[b][:, k * S + t * P:k * S + (t + 1) * P], src[:, t, k * P:(k + 1) * P])
                m.then_inc(t_full, 1)

            def values(i, h, v):
                dst = bank[7][HD * h:HD * (h + 1), :]
                pe.matmul(dst[:, S:2 * S], v[0], pT[:, i % 2, h, 0:S], start=True, stop=False)
                return pe.matmul(dst[:, S + P:2 * S], v[1], pT[:, i % 2, h, S:3 * P], start=False, stop=True)

            def mixer_step(k):
                if k in PREP_AT:
                    p = PREP_AT[k]
                    _, what, col, b = PREP[p]
                    if p == 0:
                        pe.wait_ge(emptied["dve"], N_QKV)
                    if p >= 2:
                        pe.wait_ge(prep_done, p - 1)
                    if p == 6:
                        pe.wait_ge(scores_sb, CMP + 1)
                    if p == 9:
                        pe.wait_ge(scores_sb, N_SOFT)
                    dst = bank[4 + b]
                    if what == "q":
                        if b == 0:
                            pe.wait_ge(q_rows_ready, 1 if col == QC else 2)
                        for a in range(2):
                            for t in range(TT):
                                m = transpose(dst[:, a * S + t * P:a * S + (t + 1) * P],
                                              q_rows[:, t, 2 * b + a, :, :].rearrange("p a d -> p (a d)"))
                    elif what in ("sq", "sk"):
                        for a in range(2):
                            for t in range(TT):
                                c = col + P * (2 * b + a)
                                m = transpose(dst[:, a * S + t * P:a * S + (t + 1) * P], proj[:, t, c:c + P])
                    elif what == "k":
                        for t in range(TT):
                            m = transpose(dst[:, t * P:(t + 1) * P], proj[:, t, col:col + P])
                    else:
                        for g in range(2):
                            for t in range(TT):
                                for a in range(2):
                                    c = (g * S + t * P) // 2
                                    m = pe.matmul(dst[HD * a:HD * (a + 1), c:c + P // 2],
                                                  proj[:, t, col + HD * g:col + HD * (g + 1)], ident[:, a:P:2],
                                                  start=True, stop=True)
                    m.then_inc(prep_full, 1)
                for n, end in MLP_END.items():
                    if k == end + LAG - U_MIX:
                        pe.wait_ge(emptied["act"], evac_count(mlp_q[n]))
                        for a in range(2):
                            m = transpose(bank[6][:, a * P:(a + 1) * P], hid[:, a * P:(a + 1) * P])
                        m.then_inc(hidT_full, 1)
                    if k == end + 2 * LAG - U_MIX:
                        pe.wait_ge(w2_ready, 48)
                        pe.wait_ge(hidT_ready, n + 1)
                        if n == 1:
                            pe.wait_ge(cmp_ready, 1)
                        for a in range(2):
                            if n == 0:
                                m = pe.matmul(bank[7][:, 0:32], w2k[:, a, :, :].rearrange("p r d -> p (r d)"),
                                              hid_k[:, a, :, :].rearrange("p g n -> p (g n)"),
                                              start=a == 0, stop=a == 1)
                            else:
                                m = pe.matmul(bank[7][:, 0:HD], hid_v[:, a, :, :, :].rearrange("p r g n -> p (r g n)"),
                                              w2v[:, a, :], start=a == 0, stop=a == 1)
                        m.then_inc(mlp_down, 1)
                if k in SOFT_AT:
                    i = SOFT_AT[k]
                    kind, pr = soft(i)
                    pe.wait_ge(prep_done, 6 if i <= CMP else 9)
                    if i >= 1:
                        pe.wait_ge(scores_sb, i)
                    if kind == "cmp":
                        for pr in range(PAIRS):
                            for t in range(TT):
                                m = pe.matmul(bank[4][:, t * P + 32 * pr:t * P + 32 * (pr + 1)],
                                              qT[:, pr, t * P:(t + 1) * P],
                                              kcz[:, :, :].rearrange("p a n -> p (a n)"),
                                              start=True, stop=True)
                    else:
                        keys = kz[1 if kind == "win" else 0]
                        pe.matmul(bank[5][:, 0:S], qT[:, pr, 0:P], keys[:, :, 0:P], start=True, stop=True)
                        m = pe.matmul(bank[4][:, :], qT[:, pr, P:S], keys, start=True, stop=True)
                    m.then_inc(scores_full, 1)
                if k in PROBS_T_AT:
                    i = PROBS_T_AT[k]
                    pe.wait_ge(probs, i + 1)
                    if i == 0:
                        pe.wait_ge(cmp_ready, 2)
                    else:
                        pe.wait_ge(values_read, i)
                    if soft(i)[0] == "cmp":
                        for t in range(TT):
                            m = transpose(bank[6][:, t * P:(t + 1) * P], sc[:, i % 2, 0, t * P:(t + 1) * P])
                    else:
                        for h in range(2):
                            transpose(bank[7][:, h * P:(h + 1) * P], sc[:, i % 2, h, 0:P])
                            for n in range(2):
                                m = transpose(bank[6][:, (2 * h + n) * P:(2 * h + n + 1) * P],
                                              sc[:, i % 2, h, (1 + n) * P:(2 + n) * P])
                    m.then_inc(probsT_full, 1)
                if k in VALUES_AT:
                    i = VALUES_AT[k]
                    kind, pr = soft(i)
                    pe.wait_ge(probsT, i + 1)
                    if kind == "cmp":
                        for pr in range(PAIRS):
                            m = pe.matmul(bank[7 - pr // 2][:, (pr % 2) * S:(pr % 2 + 1) * S],
                                          vz[:, 2 * pr:2 * pr + 2, :].rearrange("p h d -> p (h d)"),
                                          pT[:, i % 2, 0, 0:S], start=True, stop=True)
                    else:
                        for h in range(2):
                            c = {"sel": VSEL, "win": VWIN, "swa": VA}[kind] + HD * h
                            m = values(i, h, [proj[:, t, c:c + HD] for t in range(TT)])
                    m.then_inc(values_full, 1)
                for h, s in STICK.get(k, []):
                    if s == 0:
                        pe.wait_ge(prep_done, len(PREP))
                        if h >= 2:
                            pe.wait_ge(z_ready, h - 1)
                        dst = bank[4 + h % 2]
                        pe.matmul(dst[:, 0:S], skT[:, h, 0:P], sqT[:, h, :], start=True, stop=True)
                        pe.matmul(dst[:, S:3 * P], skT[:, h, P:S], sqT[:, h, P:S], start=True,
                                  stop=True).then_inc(z_full, 1)
                    if s == 5:
                        pe.wait_ge(z_spm, h + 1)
                        pe.wait_ge(consts_ready, 1)
                        if h >= 1:
                            pe.wait_ge(z_arg, h)
                        pe.matmul(bank[6][:, 0:3 * P], later[:, :], s_sp, start=True, stop=False)
                        pe.matmul(bank[6][:, P:S], ones[:, :], s_sp[:, S:3 * P], start=False,
                                  stop=True).then_inc(z_cum, 1)
                    if s == 9:
                        pe.wait_ge(z_w, h + 1)
                        pe.wait_ge(values_read, N_SOFT + h)
                        pe.matmul(bank[7][:, 0:S], proj[:, 0, VB + P * h:VB + P * (h + 1)], s_w[:, 0:S],
                                  start=True, stop=False)
                        pe.matmul(bank[7][:, P:S], proj[:, 1, VB + P * h:VB + P * (h + 1)], s_w[:, S:3 * P],
                                  start=False, stop=True).then_inc(z_val, 1)

            def follow(u):
                mixer_step(u - U_MIX)
                for m in range(NC_D):
                    if u == merge_T_at(m):
                        pe.wait_ge(emptied["dve"], evac_count(branch_q[2 * NC_D + m]))
                        for g in range(2):
                            n = UPC + 2 * m + g
                            if n >= UPC + 2:
                                pe.wait_ge(t_lo, n - 1)
                            else:
                                pe.wait_ge(z_ready, SB_HEADS)
                            transposes_of_rows(n, 4 + g, merged[:, :, (4 * m + 2 * g) * P:(4 * m + 2 * g + 2) * P])
                    if u == out_T_at(m):
                        pe.wait_ge(emptied["dve"], evac_count(out_q[m]))
                        for g in range(2):
                            n = 2 * UPC + 2 * m + g
                            pe.wait_ge(t_lo, n - 1)
                            transposes_of_rows(n, 4 + g, X[:, :, (4 * m + 2 * g) * P:(4 * m + 2 * g + 2) * P])

            def act_transposes(count):
                for t in range(TT):
                    pe.wait_ge(act_full, count * TT - (TT - 1 - t))
                    for g in range(2):
                        for k in range(UK):
                            m = transpose(bank[4 + g][:, k * S + t * P:k * S + (t + 1) * P],
                                          act_rows[:, t, (2 * g + k) * P:(2 * g + k + 1) * P])
                        if t == TT - 1:
                            m.then_inc(aT_full, 1)

            pe.wait_ge(ident_ready, 1)
            def warm_up(n):
                for _ in range(n):
                    transpose(bank[7][:, 0:P], ident[:, :])

            warm_up(12)
            pe.wait_ge(norm_row_ready, 16)
            transpose(bank[2][:, 0:KD], rows[0:KD, 0, :], KD).then_inc(gains_full, 1)

            def x_transposes(m):
                pe.wait_ge(x_ready[m if m < 2 else m // 2 + 1], 16)
                if m >= 4:
                    pe.wait_ge(t_lo, m - 3)
                transposes_of_rows(m, 4 + m % 4, X[:, :, 2 * m * P:(2 * m + 2) * P])

            for m in range(2):
                x_transposes(m)
            warm_up(5)
            for u in range(UPC):
                straight(u)
                for m in range(2, 4) if u == 0 else range(u + 3, min(u + 4, UPC)):
                    x_transposes(m)
                if u == 3:
                    pe.wait_ge(rows_ready, 48)
                    pe.wait_ge(gains_ready, 1)
                    for a in range(1, 4):
                        m = transpose(bank[2][:, KD * a:KD * (a + 1)], rows[0:KD, a, :], KD)
                    m.then_inc(gains_full, 1)
            with pe.Fori(0, (N_QKV - 2) // 2) as i:
                for c in range(2):
                    q0 = 1 + c
                    if c == 0:
                        pe.wait_ge(squares, 2 * NC_D)
                    for j in range(UPC):
                        u0 = UPC * q0 + j
                        pe.wait_ge(lo_ready, i * (2 * UPC) + (u0 + 1))
                        products(u0 % RING, (hT_hi, hT_lo), q0 % 2, j == 0, j == UPC - 1,
                                 UK * j, WQ).then_inc(unit_used, 1)
            for u in range(U_MIX - UPC, U_FFN):
                straight(u)
                follow(u)
            for c in range(2):
                q = Q_FFN + c
                pair_free(q)
                for j in range(UPC):
                    u = U_FFN + c * UPC + j
                    if c == 0:
                        pe.wait_ge(t_lo, 2 * UPC + j + 1)
                    unit(u, (h2T_hi, h2T_lo), q, j, UPC)
                    if u == out_T_at(NC_D - 1):
                        follow(u)
            with pe.Fori(1, NC_F) as i:
                for c in range(2):
                    if c == 0:
                        pe.wait_ge(emptied["act"], i + (evac_count(Q_FFN) - 1))
                    else:
                        pe.wait_ge(act_full, i * TT)
                    for j in range(UPC):
                        u0 = U_FFN + c * UPC + j
                        pe.wait_ge(lo_ready, i * (2 * UPC) + (u0 + 1))
                        products(u0 % RING, (h2T_hi, h2T_lo), (Q_FFN + c) % 2, j == 0, j == UPC - 1,
                                 UK * j, half=c == 1 and j == UPC - 1).then_inc(unit_used, 1)
                        if c == 0 and j == 4:
                            act_transposes(i)
            act_transposes(NC_F)
            with pe.Fori(0, NC_D // 2) as i:
                for c in range(2):
                    q = Q_DOWN + c
                    if c == 0:
                        pe.wait_ge(emptied["act"], evac_count(Q_DOWN - 2))
                    else:
                        pe.wait_ge(act_full, NC_F * TT)
                    for j in range(UPD - RING):
                        u0 = U_DOWN + c * UPD + j
                        pe.wait_ge(lo_ready, i * (2 * UPD) + (u0 + 1))
                        products(u0 % RING, (actT_hi, actT_lo), q % 2, j == 0, False, UK * j).then_inc(unit_used, 1)
                    for t in range(TT):
                        for j in range(UPD - RING, UPD):
                            u0 = U_DOWN + c * UPD + j
                            if c == 0 and t == 0 and j == UPD - 2:
                                pe.wait_ge(aT_lo, 2 * NC_F)
                            if t == 0:
                                pe.wait_ge(lo_ready, i * (2 * UPD) + (u0 + 1))
                            m = products(u0 % RING, (actT_hi, actT_lo), q % 2, False, j == UPD - 1, UK * j, tiles=(t,))
                            if t == TT - 1:
                                m.then_inc(unit_used, 1)
                        if t == 0:
                            m.then_inc(tile0_full, 1)

        @block.scalar
        def _(act):
            def split(u):
                s = u % RING
                act.wait_ge(raw_ready[s], landed(u))
                if u >= RING:
                    act.wait_ge(unit_used, u - RING + 1)
                act.activation(whi[:, s, :, 0:width(u)], raw[:, s, :, 0:width(u)], ACT.Copy).then_inc(hi_ready, 1)

            def split_in_loop(u0, rounds, units, cols=W):
                s = u0 % RING
                act.wait_ge(raw_ready[s], rounds * 16 + landed(u0))
                act.wait_ge(unit_used, units + (u0 - RING + 1))
                act.activation(whi[:, s, :, 0:cols], raw[:, s, :, 0:cols], ACT.Copy).then_inc(hi_ready, 1)

            def hi_of_transposed(n, b, dst, gain):
                act.wait_ge(t_full, n + 1)
                src = bank[b][:, :].rearrange("p (k s) -> p k s", k=UK)
                if gain is None:
                    act.activation(dst, src, ACT.Copy).then_inc(t_hi, 1)
                else:
                    for k in range(UK):
                        last = act.activation(dst[:, k, :], src[:, k, :], ACT.Copy, scale=gain[:, k:k + 1])
                    last.then_inc(t_hi, 1)

            def square(t, c, junk, done):
                if done:
                    act.wait_ge(squares, done)
                act.activation(junk[:, :], X[:, t, c * W:(c + 1) * W], ACT.Square,
                               accum_out=sumsq[:, t, c:c + 1]).then_inc(squares, 1)

            def root(n, tiles=slice(0, TT)):
                act.wait_ge(mean_ready, n)
                act.activation(stat[:, 1, tiles], stat[:, 0, tiles], ACT.Sqrt).then_inc(root_ready, 1)

            def gate_silu(full, empty_up):
                act.wait_ge(unit_used, full)
                act.wait_ge(rstd_ready, 2)
                if empty_up is not None:
                    act.wait_ge(act_full, empty_up * TT)
                for t in range(TT):
                    last = act.activation(silu[:, t, :], bank[2 * (Q_FFN % 2) + t][:, :], ACT.Silu,
                                          scale=rstd[:, t:t + 1])
                last.then_inc(emptied["act"], 1)

            def follow(v):
                q, j = CHUNK_OF.get(v, (0, 0))
                kind, i, _, n = CHUNKS[q]
                if j == n - 1 and kind == "gate":
                    act.wait_ge(unit_used, v + 1)
                    act.wait_ge(rstd_ready, 1)
                    if i >= SIG:
                        act.wait_ge(emptied["dve"], evac_count(branch_q[i - SIG]))
                    for t in range(TT):
                        last = act.activation(sig[:, i % SIG, t, :], bank[2 * (q % 2) + t][:, :], ACT.Sigmoid,
                                              scale=rstd[:, t:t + 1])
                    last.then_inc(emptied["act"], 1)
                if j == n - 1 and kind == "mlp":
                    act.wait_ge(unit_used, v + 1)
                    if i == 1:
                        act.wait_ge(hidT_full, 1)
                    act.activation(hid[:, :], bank[2 * (q % 2)][:, 0:MLP_W], ACT.Gelu_apprx_tanh)\
                       .then_inc(emptied["act"], 1)
                if v == U_FFN + UPC - 1:
                    gate_silu(v + 1, None)
                mixer_step(v - U_MIX)
                for m in range(NC_D):
                    if v == merge_T_at(m):
                        for g in range(2):
                            hi_of_transposed(UPC + 2 * m + g, 4 + g, hT_hi[:, 4 * m + 2 * g:4 * m + 2 * g + 2, :], None)
                    if v == out_T_at(m):
                        for g in range(2):
                            k0 = 4 * m + 2 * g
                            hi_of_transposed(2 * UPC + 2 * m + g, 4 + g, h2T_hi[:, k0:k0 + 2, :],
                                             gainT[:, 1, k0:k0 + 2])
                        for t in range(TT):
                            square(t, m, bank[7], TT * NC_D + TT * m + t)

            def mixer_step(k):
                if k < 0:
                    return
                if k == NSA_GATES_SLOT:
                    act.wait_ge(emptied["dve"], N_QKV)
                    act.activation(gsig[:, :, :], proj[:, :, GC:GC + NGC], ACT.Sigmoid).then_inc(nsa_gates, 1)
                if k - 1 in SOFT_AT:
                    i = SOFT_AT[k - 1]
                    kind, pr = soft(i)
                    act.wait_ge(scores_sb, i + 1)
                    if kind == "cmp":
                        act.activation(sc[:, i % 2, 0, 0:S], sc[:, i % 2, 0, 0:S], ACT.Exp).then_inc(exps, 1)
                    else:
                        sm = small[:, i % 2, :, :, :]
                        if kind == "swa":
                            act.activation(sm[:, 3, :, :], sm[:, 2, :, :], ACT.Exp)
                        for h in range(2):
                            s = sc[:, i % 2, h, :]
                            act.activation(s[:, 0:P], s[:, 0:P], ACT.Exp, bias=sm[:, 0, 0, h:h + 1],
                                           accum_out=sm[:, 1, 0, h:h + 1])
                            last = act.activation(s[:, P:3 * P], s[:, P:3 * P], ACT.Exp, bias=sm[:, 0, 1, h:h + 1],
                                                  accum_out=sm[:, 1, 1, h:h + 1])
                        last.then_inc(exps, 1)
                if k in PROBS_T_AT:
                    i = PROBS_T_AT[k]
                    act.wait_ge(probsT_full, i + 1)
                    if soft(i)[0] == "cmp":
                        act.activation(pT[:, i % 2, 0, 0:S], bank[6][:, 0:S], ACT.Copy).then_inc(probsT, 1)
                    else:
                        act.activation(pT[:, i % 2, :, 0:P], bank[7][:, 0:S].rearrange("p (h s) -> p h s", h=2), ACT.Copy)
                        act.activation(pT[:, i % 2, :, P:3 * P], bank[6][:, :].rearrange("p (h s) -> p h s", h=2),
                                       ACT.Copy).then_inc(probsT, 1)
                for h, s in STICK.get(k - 1, []):
                    if s == 0:
                        act.wait_ge(z_ready, h + 1)
                        link(act, "act", act.activation(s_ln, s_z, ACT.Abs))
                        link(act, "act", act.activation(s_ln, s_ln, ACT.Exp, scale=-1.0))
                        act.activation(s_ln, s_ln, ACT.Ln, bias=1.0).then_inc(z_ln, 1)
                    if s == 5:
                        act.wait_ge(z_arg, h + 1)
                        if h >= 1:
                            act.wait_ge(z_w, h)
                        act.activation(s_surv, s_arg, ACT.Exp).then_inc(z_surv, 1)

            act.dma_start(rows[0:KD, 0, :], norm_mix.rearrange("(k p) -> k p", p=P)).then_inc(norm_row_ready, 16)

            def gains(n, a):
                act.wait_ge(gains_full, n)
                src = bank[2][:, KD * a.start:KD * a.stop].rearrange("p (a k) -> p a k", k=KD)
                act.activation(gainT[:, a, :], src, ACT.Copy).then_inc(gains_ready, 1)
                act.wait_ge(gains_ready, n)

            act.wait_ge(ident_ready, 1)
            link(act, "act", act.activation(stat[:, 5, :], ident[:, 0:TT], ACT.Copy))
            gains(1, slice(0, 1))
            for m in range(UPC):
                hi_of_transposed(m, 4 + m % 4, hT_hi[:, 2 * m:2 * m + 2, :], gainT[:, 0, 2 * m:2 * m + 2])
                split(m)
                for n in {0: (), 1: (0, 1), 2: (2,), 3: (3, 4), 4: (5,), 5: (6,), 6: (7,)}.get(m, ()):
                    act.wait_ge(x_ready[n // 2 + 1], 16)
                    square(n % 2, n // 2, bank[3], n)
                if m == 5:
                    gains(2, slice(1, 4))
            root(1)
            with act.Fori(0, (N_QKV - 2) // 2) as i:
                for j in range(2 * UPC):
                    split_in_loop(UPC + j, i * (2 * UPC // RING), i * (2 * UPC), WQ)
            for u in range(U_MIX - UPC, U_FFN + 2 * UPC + LAG):
                split(u)
                follow(u - LAG)
                if u - LAG == out_T_at(NC_D - 1):
                    root(2)
            with act.Fori(1, NC_F) as i:
                for j in range(2 * UPC):
                    split_in_loop(U_FFN + LAG + j, i * (2 * UPC // RING), i * (2 * UPC))
                    if j == UPC - 1:
                        gate_silu(i * (2 * UPC) + (U_FFN + UPC), i)

            def split_run(u, n):
                with act.Fori(0, n // RING) as i:
                    for j in range(RING):
                        split_in_loop(u + j, i, i * RING)
                for j in range(n // RING * RING, n):
                    split(u + j)

            for c in range(NC_D):
                u = U_DOWN + c * UPD + LAG
                split_run(u, min(UPD, U_END - u))
                if c == NC_D - 1:
                    act.activation(stat[:, 5, :], ident[:, 0:TT], ACT.Sqrt)
                for t in range(TT):
                    act.wait_ge(added, TT * c + t + 1)
                    square(t, c, bank[7], 2 * TT * NC_D + TT * c + t)
                    if c == NC_D - 1:
                        root(3 + t, slice(t, t + 1))
                        act.wait_ge(rstd_ready, 3 + t)
                        for n in ACT_OUT[t]:
                            act.wait_ge(gained, n + 1)
                            piece = X[:, t, n * W:(n + 1) * W]
                            act.activation(piece, piece, ACT.Copy, scale=rstd[:, t:t + 1]).then_inc(scaled["act"], 1)

        @block.vector
        def _(dve):
            def chain(ins):
                link(dve, "dve", ins)

            def split_unit(slot, count, cols=W):
                dve.wait_ge(hi_ready, count)
                lo, w, hi = (m[:, slot, :, 0:cols] for m in (wlo, raw, whi))
                dve.tensor_tensor(lo, w, hi.bitcast(F32), ALU.subtract).then_inc(lo_ready, 1)

            def split(u):
                split_unit(u % RING, u + 1, width(u))

            def lo_of_transposed(n, b, lo, hi, gain):
                dve.wait_ge(t_hi, n + 1)
                src = bank[b][:, :].rearrange("p (k s) -> p k s", k=UK)
                if gain is None:
                    dve.tensor_tensor(lo, src, hi.bitcast(F32), ALU.subtract).then_inc(t_lo, 1)
                else:
                    for k in range(UK):
                        last = dve.scalar_tensor_tensor(lo[:, k, :], src[:, k, :], gain[:, k:k + 1],
                                                        hi[:, k, :].bitcast(F32), ALU.mult, ALU.subtract)
                    last.then_inc(t_lo, 1)

            def norm(n, done, tiles=slice(0, TT)):
                dve.wait_ge(squares, done)
                total, mean, root, y, z = (stat[:, r, tiles] for r in (2, 0, 1, 3, 4))
                chain(dve.tensor_reduce(out=total, in_=sumsq[:, tiles, :], axis=AX_X, op=ALU.add))
                dve.tensor_scalar(mean, total, 1.0 / D, EPS, ALU.mult, ALU.add).then_inc(mean_ready, 1)
                dve.wait_ge(root_ready, n)
                chain(dve.reciprocal(y, root))
                for t in range(tiles.start, tiles.stop):
                    y_t = stat[:, 3, t:t + 1]
                    last = dve.scalar_tensor_tensor(stat[:, 4, t:t + 1], y_t, stat[:, 0, t:t + 1], y_t, ALU.mult, ALU.mult)
                chain(last)
                chain(dve.tensor_scalar(z, z, -0.5, 1.5, ALU.mult, ALU.add))
                dve.tensor_tensor(rstd[:, tiles], y, z, ALU.mult).then_inc(rstd_ready, 1)

            def split_y(r, k, src):
                chain(dve.tensor_copy(yT_hi[:, r, k, :], src))
                return dve.tensor_tensor(yT_lo[:, r, k, :], src, yT_hi[:, r, k, :].bitcast(F32), ALU.subtract)

            def empty_projection(pair, cols, w=WQ):
                for t in range(TT):
                    last = dve.tensor_scalar(proj[:, t, cols], bank[2 * pair + t][:, 0:w], rstd[:, t:t + 1], None, ALU.mult)
                last.then_inc(emptied["dve"], 1)

            def follow(v):
                q, j = CHUNK_OF.get(v, (0, 0))
                kind, i, _, n = CHUNKS[q]
                pair = q % 2
                if j == n - 1 and kind == "qkv":
                    dve.wait_ge(unit_used, v + 1)
                    empty_projection(pair, slice(i * WQ, min((i + 1) * WQ, N_PROJ)), width(v))
                if j == n - 1 and kind == "branch":
                    s, c = i // NC_D, i % NC_D
                    dve.wait_ge(unit_used, v + 1)
                    dve.wait_ge(emptied["act"], evac_count(gate_q[i]))
                    cols = slice(c * W, (c + 1) * W)
                    for t in range(TT):
                        dst = merged[:, t, cols] if s == 0 else sig[:, i % SIG, t, :]
                        last = dve.tensor_tensor(dst, bank[2 * pair + t][:, :], sig[:, i % SIG, t, :], ALU.mult)
                    if s > 0:
                        chain(last)
                        last = dve.tensor_tensor(merged[:, :, cols], merged[:, :, cols], sig[:, i % SIG, :, :], ALU.add)
                    last.then_inc(emptied["dve"], 1)
                if j == n - 1 and kind == "out":
                    dve.wait_ge(unit_used, v + 1)
                    dve.wait_ge(x_again, 16)
                    for t in range(TT):
                        last = dve.tensor_tensor(X[:, t, i * W:(i + 1) * W], bank[2 * pair + t][:, :],
                                                 X[:, t, i * W:(i + 1) * W], ALU.add)
                    last.then_inc(emptied["dve"], 1)
                if v == U_FFN + 2 * UPC - 1:
                    gated(v + 1, 1, evac_count(Q_FFN))
                mixer_step(v - U_MIX)
                for m in range(NC_D):
                    for g in range(2):
                        k0 = 4 * m + 2 * g
                        if v == merge_T_at(m):
                            lo_of_transposed(UPC + 2 * m + g, 4 + g, hT_lo[:, k0:k0 + 2, :], hT_hi[:, k0:k0 + 2, :], None)
                        if v == out_T_at(m):
                            lo_of_transposed(2 * UPC + 2 * m + g, 4 + g, h2T_lo[:, k0:k0 + 2, :],
                                             h2T_hi[:, k0:k0 + 2, :], gainT[:, 1, k0:k0 + 2])

            def prepare(p):
                _, what, col, b = PREP[p]
                dve.wait_ge(prep_full, p + 1)
                src = bank[4 + b][:, :].rearrange("p (a s) -> p a s", a=2)
                if what == "q":
                    last = dve.tensor_scalar(qT[:, 2 * b:2 * b + 2, :], src, SCALE, None, ALU.mult)
                elif what == "sq":
                    last = dve.tensor_copy(sqT[:, 2 * b:2 * b + 2, :], src)
                elif what == "sk":
                    last = dve.tensor_copy(skT[:, 2 * b:2 * b + 2, :], src)
                elif what == "k":
                    dst = kz[1 if col == KWIN else 0]
                    for a in range(2):
                        half = slice(HD * a, HD * (a + 1))
                        last = dve.tensor_copy(dst[half, a, :], src[half, 0, :])
                else:
                    m = 0 if col == KCMP else 1
                    for a in range(2):
                        half = slice(HD * a, HD * (a + 1))
                        for g in range(2):
                            tok = src[half, 0, g * P:(g + 1) * P].rearrange("p (n s) -> p s n", s=8)
                            for e in range(2):
                                ks = slice(8 * e, 8 * e + 8)
                                last = dve.tensor_tensor(
                                    blkT[half, ks, m, NP_CMP * g:NP_CMP * g + N_CMP], tok[:, :, e:e + N_CMP],
                                    gainT[half, 2 + m, ks].unsqueeze(2).to_broadcast([HD, 8, N_CMP]), ALU.add)
                last.then_inc(prep_done, 1)

            def split_blocks():
                dve.wait_ge(prep_done, 2)
                hi, lo = (b[:, :, 0:4 * NP_CMP].rearrange("p k (m c) -> p k m c", m=2) for b in (blk_hi, blk_lo))
                chain(dve.tensor_copy(hi, blkT))
                dve.tensor_tensor(lo, blkT, hi.bitcast(F32), ALU.subtract).then_inc(blk_ready, 1)

            def masked_scores(i):
                kind, pr = soft(i)
                dve.wait_ge(scores_full, i + 1)
                if i >= 2:
                    dve.wait_ge(probsT_full, i - 1)
                if kind == "cmp":
                    s = sc[:, i % 2, 0, 0:S].rearrange("p (q h n) -> p q h n", q=TT, h=HEADS)
                    chain(dve.tensor_tensor(sc[:, i % 2, 0, 0:S], bank[4][:, 0:S],
                                            bias_c[:, :, :, :].rearrange("p q h n -> p (q h n)"), ALU.add))
                    chain(dve.tensor_reduce(out=csum[:, 0, :, :], in_=s, axis=AX_X, op=ALU.max))
                    dve.tensor_tensor(s, s, csum[:, 0, :, :].unsqueeze(3).to_broadcast([P, TT, HEADS, NP_CMP]),
                                      ALU.subtract).then_inc(scores_sb, 1)
                    return
                s, sm = sc[:, i % 2, :, :], small[:, i % 2, :, :, :]
                table = negdist_w if kind == "swa" else negdist
                for h in range(2):
                    dve.scalar_tensor_tensor(s[:, h, 0:P], table[:, P:S], slope(head(pr, h)),
                                             bank[5][:, h * P:(h + 1) * P], ALU.mult, ALU.add)
                    last = dve.scalar_tensor_tensor(s[:, h, P:3 * P], table[:, :], slope(head(pr, h)),
                                                    bank[4][:, h * S:(h + 1) * S], ALU.mult, ALU.add)
                chain(last)
                dve.tensor_reduce(out=sm[:, 0, 0, :], in_=s[:, :, 0:P], axis=AX_X, op=ALU.max, negate=True)
                last = dve.tensor_reduce(out=sm[:, 0, 1, :], in_=s[:, :, P:3 * P], axis=AX_X, op=ALU.max, negate=True)
                if kind == "swa":
                    chain(last)
                    sk = sinkb[:, pr:HEADS:PAIRS]
                    for t in range(TT):
                        last = dve.scalar_tensor_tensor(sm[:, 0, t, :], sk, -1.0, sm[:, 0, t, :], ALU.mult, ALU.min)
                    chain(last)
                    for t in range(TT):
                        last = dve.tensor_tensor(sm[:, 2, t, :], sk, sm[:, 0, t, :], ALU.add)
                last.then_inc(scores_sb, 1)

            def normalised(i):
                kind, pr = soft(i)
                dve.wait_ge(exps, i + 1)
                if kind == "cmp":
                    s = sc[:, i % 2, 0, 0:S].rearrange("p (q h n) -> p q h n", q=TT, h=HEADS)
                    valid = valid_c[:, :, :].unsqueeze(2).to_broadcast([P, TT, HEADS, NP_CMP])
                    chain(dve.tensor_tensor(s, s, valid, ALU.mult))
                    chain(dve.tensor_reduce(out=csum[:, 0, :, :], in_=s, axis=AX_X, op=ALU.add))
                    chain(dve.tensor_scalar(csum[:, 1, :, :], csum[:, 0, :, :], 1e-30, None, ALU.max))
                    chain(dve.reciprocal(csum[:, 2, :, :], csum[:, 1, :, :]))
                    gate = gsig[:, :, :].rearrange("p t (a r b) -> p t r a b", a=2, b=3)[:, :, :, :, 0]
                    res, inv = (csum[:, n, :, :].rearrange("p t (r a) -> p t r a", a=2) for n in (0, 2))
                    for t in range(TT):
                        last = dve.tensor_tensor(res[:, t, :, :], inv[:, t, :, :], gate[:, t, :, :], ALU.mult)
                    chain(last)
                    dve.tensor_tensor(s, s, csum[:, 0, :, :].unsqueeze(3).to_broadcast([P, TT, HEADS, NP_CMP]),
                                      ALU.mult).then_inc(probs, 1)
                    return
                s, sm = sc[:, i % 2, :, :], small[:, i % 2, :, :, :]
                if kind == "swa":
                    chain(dve.tensor_tensor(sm[:, 1, :, :], sm[:, 1, :, :], sm[:, 3, :, :], ALU.add))
                    chain(dve.reciprocal(sm[:, 5, :, :], sm[:, 1, :, :]))
                else:
                    chain(dve.reciprocal(sm[:, 4, :, :], sm[:, 1, :, :]))
                    b = 1 if kind == "sel" else 2
                    gate = gsig[:, :, :].rearrange("p t (h b) -> p t h b", b=3)[:, :, pr:HEADS:PAIRS, b]
                    chain(dve.tensor_tensor(sm[:, 5, :, :], sm[:, 4, :, :], gate, ALU.mult))
                for h in range(2):
                    dve.tensor_scalar(s[:, h, 0:P], s[:, h, 0:P], sm[:, 5, 0, h:h + 1], None, ALU.mult)
                    last = dve.tensor_scalar(s[:, h, P:3 * P], s[:, h, P:3 * P], sm[:, 5, 1, h:h + 1], None, ALU.mult)
                last.then_inc(probs, 1)

            def read_values(i):
                kind, pr = soft(i)
                dve.wait_ge(values_full, i + 1)
                src = bank[7][:, S:2 * S]
                if kind == "sel":
                    last = dve.tensor_copy(yacc[:, pr, :], src)
                elif kind == "win":
                    last = dve.tensor_tensor(yacc[:, pr, :], src, yacc[:, pr, :], ALU.add)
                elif kind == "swa":
                    last = split_y(1, pr, src)
                else:
                    for n in range(2):
                        acc = yacc[:, 2 * n:2 * n + 2, :]
                        chain(dve.tensor_tensor(acc, bank[7 - n][:, :].rearrange("p (a s) -> p a s", a=2), acc, ALU.add))
                        last = split_y(0, slice(2 * n, 2 * n + 2), acc)
                last.then_inc(values_read, 1)

            def mixer_step(k):
                if k < 0:
                    return
                if k in PREP_AT:
                    prepare(PREP_AT[k])
                if k == 1:
                    split_blocks()
                for n, end in MLP_END.items():
                    if k == end + LAG - U_MIX:
                        dve.wait_ge(hidT_full, n + 1)
                        src = bank[6][:, 0:S].rearrange("p (a c) -> p a c", a=2)[:, :, 2 * n * NP_CMP:2 * (n + 1) * NP_CMP]
                        src = src.rearrange("p a (g n) -> p a g n", g=2)
                        if n == 0:
                            dve.tensor_copy(hid_k[:, :, :, :], src).then_inc(hidT_ready, 1)
                        else:
                            for r in range(PAIRS):
                                last = dve.tensor_copy(hid_v[:, :, r, :, :], src)
                            last.then_inc(hidT_ready, 1)
                    if k == end + 2 * LAG - U_MIX:
                        dve.wait_ge(mlp_down, n + 1)
                        if n == 0:
                            for a in range(2):
                                half = slice(HD * a, HD * (a + 1))
                                last = dve.tensor_copy(kcz[half, a, :], bank[7][half, a * NP_CMP:(a + 1) * NP_CMP])
                        else:
                            last = dve.tensor_tensor(vz[:, :, :], bank[7][:, 0:HD].unsqueeze(1).to_broadcast([P, HEADS, HD]),
                                                     head_mask[:, :].unsqueeze(2).to_broadcast([P, HEADS, HD]), ALU.mult)
                        last.then_inc(cmp_ready, 1)
                if k in SOFT_AT:
                    masked_scores(SOFT_AT[k])
                if k - 2 in SOFT_AT:
                    normalised(SOFT_AT[k - 2])
                if k in VALUES_AT:
                    read_values(VALUES_AT[k])
                for h, s in STICK.get(k, []):
                    if s == 0:
                        dve.wait_ge(z_full, h + 1)
                        if h >= 1:
                            dve.wait_ge(z_arg, h)
                        dve.tensor_scalar(s_z, bank[4 + h % 2][:, 0:3 * P], SB_SCALE, None, ALU.mult).then_inc(z_ready, 1)
                    if s == 5:
                        dve.wait_ge(z_cum, h + 1)
                        if h >= 1:
                            dve.wait_ge(z_surv, h)
                        dve.tensor_tensor(s_arg, s_z, bank[6][:, 0:3 * P], ALU.subtract).then_inc(z_arg, 1)
                    if s == 9:
                        dve.wait_ge(z_val, h + 1)
                        if h == 0:
                            dve.wait_ge(unit_used, BRANCH_END[NC_D - 1] + 1)
                        last = split_y(0, h, bank[7][:, 0:S])
                        last.then_inc(values_read, 1)
                for h, s in STICK.get(k - 2, []):
                    if s == 0:
                        dve.wait_ge(z_ln, h + 1)
                        if h >= 1:
                            dve.wait_ge(z_cum, h)
                        dve.scalar_tensor_tensor(s_sp, s_z, 0.0, s_ln, ALU.max, ALU.add).then_inc(z_sp, 1)
                        chain(dve.scalar_tensor_tensor(s_z, s_z, 0.0, s_ln, ALU.min, ALU.subtract))

            for m in range(UPC):
                ks = slice(2 * m, 2 * m + 2)
                lo_of_transposed(m, 4 + m % 4, hT_lo[:, ks, :], hT_hi[:, ks, :], gainT[:, 0, ks])
                split(m)
            norm(1, TT * NC_D)
            dve.wait_ge(rstd_ready, 1)
            with dve.Fori(0, (N_QKV - 2) // 2) as i:
                for c in range(2):
                    for j in range(UPC):
                        u0 = UPC + c * UPC + j
                        split_unit(u0 % RING, i * (2 * UPC) + (u0 + 1), WQ)
                        if j == LAG - 1:
                            dve.wait_ge(unit_used, i * (2 * UPC) + UPC * (1 + c))
                            empty_projection(c, bass.ds(i * (2 * WQ) + c * WQ, WQ))
            dve.wait_ge(consts_ready, 1)
            dve.wait_ge(sinks_ready, 16)

            def gated(full, count, silus):
                dve.wait_ge(emptied["act"], silus)
                for t in range(TT):
                    dve.wait_ge(tile0_full, count) if t == 0 else dve.wait_ge(unit_used, full)
                    dve.scalar_tensor_tensor(act_rows[:, t, :], bank[2 * ((Q_FFN + 1) % 2) + t][:, :],
                                                    rstd[:, t:t + 1], silu[:, t, :], ALU.mult,
                                             ALU.mult).then_inc(act_full, 1)

            for u in range(U_MIX - UPC, U_FFN + 2 * UPC + LAG):
                split(u)
                if u == U_MIX + LAG:
                    dve.wait_ge(zeros_ready, 1)
                if u == U_MIX + soft_slot(0) + 2 + LAG:
                    dve.wait_ge(nsa_gates, 1)
                follow(u - LAG)
                if u - LAG == out_T_at(NC_D - 1):
                    norm(2, 2 * TT * NC_D)
                    dve.wait_ge(rstd_ready, 2)

            def act_columns(g, done, rows_of):
                src = bank[4 + g][:, :].rearrange("p (k s) -> p k s", k=UK)
                dve.wait_ge(aT_full, done + 1)
                dve.tensor_scalar(actT_hi[:, rows_of, :], src, 1.0, None, ALU.mult).then_inc(aT_hi, 1)
                dve.wait_ge(aT_hi, done + 1)
                dve.tensor_tensor(actT_lo[:, rows_of, :], src, actT_hi[:, rows_of, :].bitcast(F32),
                                  ALU.subtract).then_inc(aT_lo, 1)

            silus = evac_count(Q_FFN)
            with dve.Fori(1, NC_F) as i:
                for j in range(2 * UPC):
                    u0 = U_FFN + LAG + j
                    split_unit(u0 % RING, i * (2 * UPC) + (u0 + 1))
                    if j in (4, 5):
                        g = j - 4
                        act_columns(g, i * 2 + (g - 2), bass.ds(i * 4 + (2 * g - 4), 2))
                    if j == 2 * UPC - 1:
                        gated(i * (2 * UPC) + (U_FFN + 2 * UPC), i + 1, i + silus)
            for g in range(2):
                act_columns(g, 2 * (NC_F - 1) + g, slice(KF - 4 + 2 * g, KF - 2 + 2 * g))

            def split_run(u, n):
                with dve.Fori(0, n // RING) as i:
                    for j in range(RING):
                        split_unit((u + j) % RING, i * RING + (u + j + 1))
                for j in range(n // RING * RING, n):
                    split(u + j)

            for c in range(NC_D):
                u = U_DOWN + c * UPD + LAG
                split_run(u, min(UPD, U_END - u))
                cols = slice(c * W, (c + 1) * W)
                for t in range(TT):
                    dve.wait_ge(tile0_full, NC_F + c + 1) if t == 0 else dve.wait_ge(unit_used, U_DOWN + (c + 1) * UPD)
                    dve.tensor_tensor(X[:, t, cols], bank[2 * ((Q_DOWN + c) % 2) + t][:, :], X[:, t, cols],
                                      ALU.add).then_inc(added, 1)
                    if c == NC_D - 1:
                        norm(3 + t, 3 * TT * NC_D - TT + t + 1, slice(t, t + 1))
                        dve.wait_ge(rstd_ready, 3 + t)
                        dve.wait_ge(gfin_ready, 16)
                        for n in DVE_OUT[t]:
                            piece = X[:, t, n * W:(n + 1) * W]
                            if n == NC_D - 1:
                                last = dve.scalar_tensor_tensor(piece, piece, rstd[:, t:t + 1], gfin[:, D - W:D],
                                                                ALU.mult, ALU.mult)
                            else:
                                dve.wait_ge(gained, n + 1)
                                last = dve.tensor_scalar(piece, piece, rstd[:, t:t + 1], None, ALU.mult)
                            last.then_inc(scaled["dve"], 1)


_OUT = (1, S, D)


def kernel(x, norm_mix, w_in, swa_sinks, cmp_pe_k, cmp_w1_k, cmp_w2_k, cmp_pe_v, cmp_w1_v, cmp_w2_v,
           w_branch_swa, w_branch_sb, w_branch_nsa, w_out, norm_ffn, w_gate, w_up, w_down, norm_final):
    import numpy as np
    import concourse.bacc as bacc
    from concourse.bass_utils import run_bass_kernel_spmd

    arrays = {
        "x": x, "norm_mix": norm_mix, "w_in": w_in, "sinks": swa_sinks,
        "pe_k": cmp_pe_k, "w1_k": cmp_w1_k, "w2_k": cmp_w2_k, "pe_v": cmp_pe_v, "w1_v": cmp_w1_v, "w2_v": cmp_w2_v,
        "w_br_a": w_branch_swa, "w_br_b": w_branch_sb, "w_br_c": w_branch_nsa, "w_out": w_out,
        "norm_ffn": norm_ffn, "w_gate": w_gate, "w_up": w_up, "w_down": w_down, "norm_final": norm_final,
    }
    arrays = {"in_" + k: np.ascontiguousarray(v) for k, v in arrays.items()}
    nc = bacc.Bacc("TRN2", target_bir_lowering=False, num_devices=1)
    args = []
    for name, a in arrays.items():
        ap = nc.dram_tensor(name, a.shape, mybir.dt.from_np(a.dtype), kind="ExternalInput").ap()
        args.append(ap if name == "in_norm_final" else ap[0])
    res = nc.dram_tensor("out", _OUT, F32, kind="ExternalOutput").ap()
    build_layer(nc, *args, res[0])
    r = run_bass_kernel_spmd(nc, [arrays], core_ids=[0])
    return r.results[0]["out"]
```
